# Optimizing a Trainium2 kernel written in Bass

```python
import math
import jax, jax.numpy as jnp
from jax import lax
import numpy as np

D_MODEL = 1024
BATCH = 1
SEQ = 256
DEPTH = 2

MEM_LEN = 256
MLA_HEADS = 8
MLA_NOPE_DIM = 64
MLA_ROPE_DIM = 32
MLA_V_DIM = 64
Q_LORA_RANK = 384
KV_LORA_RANK = 256
ROPE_THETA = 10000.0
DIL_HEADS = 8
DIL_HEAD_DIM = 64
DIL_PATTERNS = ((128, 1), (512, 4), (2048, 16))
N_BUCKETS = 32
MAX_DISTANCE = 2048
X_HEADS = 4
X_HEAD_DIM = D_MODEL // X_HEADS
D_FF = 4 * D_MODEL

Q_BLOCK = 128
EPS = 1e-6
MLA_WIDTH = MLA_HEADS * MLA_V_DIM
DIL_WIDTH = DIL_HEADS * DIL_HEAD_DIM
MIX_WIDTH = MLA_WIDTH + DIL_WIDTH
MLA_QK_DIM = MLA_NOPE_DIM + MLA_ROPE_DIM
IN_WIDTH = Q_LORA_RANK + KV_LORA_RANK + MLA_ROPE_DIM + 3 * DIL_WIDTH


def rms_norm(x, g):
    xf = x.astype(jnp.float32)
    y = xf * lax.rsqrt(jnp.mean(xf * xf, axis=-1, keepdims=True) + EPS)
    return (y * g.astype(jnp.float32)).astype(x.dtype)

def rope(x, positions):
    half = x.shape[-1] // 2
    inv = ROPE_THETA ** (-jnp.arange(half, dtype=jnp.float32) / half)
    ang = positions.astype(jnp.float32)[..., None] * inv
    cos = jnp.cos(ang)[:, :, None, :]
    sin = jnp.sin(ang)[:, :, None, :]
    x1 = x[..., :half].astype(jnp.float32)
    x2 = x[..., half:].astype(jnp.float32)
    out = jnp.concatenate([x1 * cos - x2 * sin, x2 * cos + x1 * sin], axis=-1)
    return out.astype(x.dtype)

def t5_bucket(dist):
    max_exact = N_BUCKETS // 2
    d = jnp.maximum(dist, 0)
    df = jnp.maximum(d.astype(jnp.float32), 1.0)
    large = max_exact + (jnp.log(df / max_exact) / math.log(MAX_DISTANCE / max_exact)
                         * (N_BUCKETS - max_exact)).astype(jnp.int32)
    large = jnp.minimum(large, N_BUCKETS - 1)
    return jnp.where(d < max_exact, d, large)

def causal_block_attention(q, k, v):
    B, S, H, Dqk = q.shape
    scale = Dqk ** -0.5
    nblk = S // Q_BLOCK
    qb = q.reshape(B, nblk, Q_BLOCK, H, Dqk).transpose(1, 0, 2, 3, 4)
    kpos = jnp.arange(S)

    def block(args):
        qi, bi = args
        s = jnp.einsum('bqhd,bkhd->bhqk', qi, k, preferred_element_type=jnp.float32) * scale
        qpos = bi * Q_BLOCK + jnp.arange(Q_BLOCK)
        s = jnp.where(kpos[None, :] <= qpos[:, None], s, -jnp.inf)
        p = jax.nn.softmax(s, axis=-1).astype(v.dtype)
        return jnp.einsum('bhqk,bkhd->bqhd', p, v)

    out = lax.map(block, (qb, jnp.arange(nblk)))
    return out.transpose(1, 0, 2, 3, 4).reshape(B, S, H, v.shape[-1])

def dilated_window_attention(q, k, v, rel_bias, window, dil):
    B, S, H, D = q.shape
    n = window // dil
    span = dil * n
    Sp = -(-S // span) * span
    L = Sp // dil
    nc = L // n
    scale = D ** -0.5

    def to_strided(t):
        t = jnp.pad(t, ((0, 0), (0, Sp - S), (0, 0), (0, 0)))
        t = t.reshape(B, L, dil, H, D)
        t = t.transpose(0, 2, 1, 3, 4)
        return t.reshape(B, dil, nc, n, H, D)

    qq, kc, vc = to_strided(q), to_strided(k), to_strided(v)

    def with_prev(t):
        prev = jnp.concatenate([jnp.zeros_like(t[:, :, :1]), t[:, :, :-1]], axis=2)
        return jnp.concatenate([prev, t], axis=3)

    kk, vv = with_prev(kc), with_prev(vc)

    i = jnp.arange(n)[:, None]
    m = jnp.arange(2 * n)[None, :]
    rel = n + i - m
    band = (rel >= 0) & (rel <= n)
    c = jnp.arange(nc)[:, None, None]
    mask = (band[None] & ((c > 0) | (m[None] >= n)))[:, None]
    bias = rel_bias.astype(jnp.float32)[t5_bucket(rel * dil)].transpose(2, 0, 1)

    s = jnp.einsum('brcqhd,brckhd->brchqk', qq, kk, preferred_element_type=jnp.float32) * scale + bias
    s = jnp.where(mask, s, -jnp.inf)
    s_max = jnp.max(s, axis=-1, keepdims=True)
    e = jnp.exp(s - s_max)
    den = jnp.sum(e, axis=-1)
    o = jnp.einsum('brchqk,brckhd->brcqhd', e, vv.astype(jnp.float32))
    den_q = den.transpose(0, 1, 2, 4, 3)
    o = o / den_q[..., None]
    lse = s_max[..., 0].transpose(0, 1, 2, 4, 3) + jnp.log(den_q)

    def from_strided(t):
        t = t.reshape((B, dil, L) + t.shape[4:])
        t = jnp.moveaxis(t, 1, 2)
        return t.reshape((B, Sp) + t.shape[3:])[:, :S]

    return from_strided(o), from_strided(lse)

def hybrid_mixer(h, positions, rel_bias, w_in, q_norm_g, w_uq, kv_norm_g, w_ukv, w_out):
    B, S, _ = h.shape
    z = h @ w_in
    o1 = Q_LORA_RANK
    o2 = o1 + KV_LORA_RANK
    o3 = o2 + MLA_ROPE_DIM
    o4 = o3 + DIL_WIDTH
    o5 = o4 + DIL_WIDTH
    c_q, c_kv, k_rope = z[..., :o1], z[..., o1:o2], z[..., o2:o3]
    q_d, k_d, v_d = z[..., o3:o4], z[..., o4:o5], z[..., o5:]

    q = (rms_norm(c_q, q_norm_g) @ w_uq).reshape(B, S, MLA_HEADS, MLA_QK_DIM)
    q = jnp.concatenate([q[..., :MLA_NOPE_DIM], rope(q[..., MLA_NOPE_DIM:], positions)], axis=-1)
    kv = (rms_norm(c_kv, kv_norm_g) @ w_ukv).reshape(B, S, MLA_HEADS, MLA_NOPE_DIM + MLA_V_DIM)
    k_nope, v_mla = kv[..., :MLA_NOPE_DIM], kv[..., MLA_NOPE_DIM:]
    k_pe = rope(k_rope[:, :, None, :], positions)
    k_pe = jnp.broadcast_to(k_pe, (B, S, MLA_HEADS, MLA_ROPE_DIM))
    k = jnp.concatenate([k_nope, k_pe], axis=-1)
    o_mla = causal_block_attention(q, k, v_mla).reshape(B, S, MLA_WIDTH)

    qd = q_d.reshape(B, S, DIL_HEADS, DIL_HEAD_DIM)
    kd = k_d.reshape(B, S, DIL_HEADS, DIL_HEAD_DIM)
    vd = v_d.reshape(B, S, DIL_HEADS, DIL_HEAD_DIM)
    outs, lses = [], []
    for window, dil in DIL_PATTERNS:
        o_p, lse_p = dilated_window_attention(qd, kd, vd, rel_bias, window, dil)
        outs.append(o_p)
        lses.append(lse_p)
    w = jax.nn.softmax(jnp.stack(lses, axis=0), axis=0)
    o_dil = jnp.sum(w[..., None] * jnp.stack(outs, axis=0), axis=0)
    o_dil = o_dil.astype(h.dtype).reshape(B, S, DIL_WIDTH)

    return jnp.concatenate([o_mla, o_dil], axis=-1) @ w_out

def memory_cross_attention(h, mem_n, w_xq, w_xk, w_xv, w_xo):
    B, S, _ = h.shape
    M = mem_n.shape[1]
    q = (h @ w_xq).reshape(B, S, X_HEADS, X_HEAD_DIM)
    k = (mem_n @ w_xk).reshape(B, M, X_HEADS, X_HEAD_DIM)
    v = (mem_n @ w_xv).reshape(B, M, X_HEADS, X_HEAD_DIM)
    s = jnp.einsum('bshd,bmhd->bhsm', q, k, preferred_element_type=jnp.float32) * (X_HEAD_DIM ** -0.5)
    p = jax.nn.softmax(s, axis=-1).astype(v.dtype)
    o = jnp.einsum('bhsm,bmhd->bshd', p, v).reshape(B, S, D_MODEL)
    return o @ w_xo

def first_inputs(seed: int = 0) -> dict:
    key = jax.random.key(seed)
    ks = jax.random.split(key, 32)

    def w(k, shape, fan_in):
        return jax.random.normal(k, shape, jnp.float32) * fan_in ** -0.5

    def gain(k, dim):
        return 1.0 + 0.05 * jax.random.normal(k, (DEPTH, dim), jnp.float32)

    offset = jax.random.randint(ks[2], (BATCH, 1), 0, 1024, dtype=jnp.int32)
    positions = offset + jnp.arange(SEQ, dtype=jnp.int32)[None, :]
    return {
        "x": jax.random.normal(ks[0], (BATCH, SEQ, D_MODEL), jnp.float32),
        "mem": jax.random.normal(ks[1], (BATCH, MEM_LEN, D_MODEL), jnp.float32),
        "positions": positions,
        "rel_bias": 0.5 * jax.random.normal(ks[3], (N_BUCKETS, DIL_HEADS), jnp.float32),
        "w_in": w(ks[4], (DEPTH, D_MODEL, IN_WIDTH), D_MODEL),
        "q_norm_g": gain(ks[5], Q_LORA_RANK),
        "w_uq": w(ks[6], (DEPTH, Q_LORA_RANK, MLA_HEADS * MLA_QK_DIM), Q_LORA_RANK),
        "kv_norm_g": gain(ks[7], KV_LORA_RANK),
        "w_ukv": w(ks[8], (DEPTH, KV_LORA_RANK, MLA_HEADS * (MLA_NOPE_DIM + MLA_V_DIM)), KV_LORA_RANK),
        "w_mix_out": w(ks[9], (DEPTH, MIX_WIDTH, D_MODEL), MIX_WIDTH),
        "pre_mix_g": gain(ks[10], D_MODEL),
        "post_mix_g": gain(ks[11], D_MODEL),
        "w_xq": w(ks[12], (DEPTH, D_MODEL, D_MODEL), D_MODEL),
        "w_xk": w(ks[13], (DEPTH, D_MODEL, D_MODEL), D_MODEL),
        "w_xv": w(ks[14], (DEPTH, D_MODEL, D_MODEL), D_MODEL),
        "w_xo": w(ks[15], (DEPTH, D_MODEL, D_MODEL), D_MODEL),
        "mem_g": gain(ks[16], D_MODEL),
        "pre_xattn_g": gain(ks[17], D_MODEL),
        "post_xattn_g": gain(ks[18], D_MODEL),
        "w_up": w(ks[19], (DEPTH, D_MODEL, D_FF), D_MODEL),
        "w_down": w(ks[20], (DEPTH, D_FF, D_MODEL), D_FF),
        "pre_mlp_g": gain(ks[21], D_MODEL),
        "post_mlp_g": gain(ks[22], D_MODEL),
    }

def first_block(x, mem, positions, rel_bias, w_in, q_norm_g, w_uq, kv_norm_g, w_ukv, w_mix_out,
              pre_mix_g, post_mix_g, w_xq, w_xk, w_xv, w_xo, mem_g, pre_xattn_g, post_xattn_g,
              w_up, w_down, pre_mlp_g, post_mlp_g):
    for l in range(DEPTH):
        a = hybrid_mixer(rms_norm(x, pre_mix_g[l]), positions, rel_bias, w_in[l], q_norm_g[l],
                         w_uq[l], kv_norm_g[l], w_ukv[l], w_mix_out[l])
        x = x + rms_norm(a, post_mix_g[l])
        c = memory_cross_attention(rms_norm(x, pre_xattn_g[l]), rms_norm(mem, mem_g[l]),
                                   w_xq[l], w_xk[l], w_xv[l], w_xo[l])
        x = x + rms_norm(c, post_xattn_g[l])
        hdn = jnp.square(jax.nn.relu(rms_norm(x, pre_mlp_g[l]) @ w_up[l]))
        x = x + rms_norm(hdn @ w_down[l], post_mlp_g[l])
    return x


DEPTH_2 = 1

D_MIX = D_MODEL
HEAD_DIM = 64
SG_WIDTH = D_MIX // 2
SG_GROUPS = SG_WIDTH // HEAD_DIM
SG_CHUNK = 128
NSA_WIDTH = D_MIX - SG_WIDTH
NSA_HEADS = NSA_WIDTH // HEAD_DIM
NSA_KV_HEADS = 2
NSA_GROUP = NSA_HEADS // NSA_KV_HEADS
KV_WIDTH = NSA_KV_HEADS * HEAD_DIM
N_BRANCH = 3
CMP_BLOCK = 32
CMP_STRIDE = 16
CMP_HIDDEN = 256
SLC_BLOCK = 64
SLC_TOPK = 16
WINDOW = 512
FORCE_SCORE = 1e4
IN_COLS = 2 * SG_WIDTH + NSA_WIDTH + 6 * KV_WIDTH + NSA_HEADS * N_BRANCH
MEM_HEADS = 4
MEM_HEAD_DIM = 128
D_FF_2 = 4 * D_MODEL


def rms_norm_2(x, g):
    xf = x.astype(jnp.float32)
    y = xf * lax.rsqrt(jnp.mean(xf * xf, axis=-1, keepdims=True) + EPS)
    return (y * g.astype(jnp.float32)).astype(x.dtype)

def layer_norm(x, g, b):
    xf = x.astype(jnp.float32)
    mu = jnp.mean(xf, axis=-1, keepdims=True)
    xc = xf - mu
    y = xc * lax.rsqrt(jnp.mean(xc * xc, axis=-1, keepdims=True) + EPS)
    return (y * g.astype(jnp.float32) + b.astype(jnp.float32)).astype(x.dtype)

def masked_softmax(s, mask):
    s = jnp.where(mask, s.astype(jnp.float32), -jnp.inf)
    m = jnp.max(s, axis=-1, keepdims=True)
    m = jnp.where(jnp.isfinite(m), m, 0.0)
    e = jnp.exp(s - m)
    d = jnp.sum(e, axis=-1, keepdims=True)
    return e / jnp.where(d > 0, d, 1.0)

def spatial_gating_unit(u, v, ln_g, ln_b, w_s, b_s):
    B, T, _ = u.shape
    v = layer_norm(v, ln_g, ln_b)
    vb = v.reshape(B, T // SG_CHUNK, SG_CHUNK, SG_GROUPS, HEAD_DIM)
    causal = jnp.tril(jnp.ones((SG_CHUNK, SG_CHUNK), dtype=bool))
    w = jnp.where(causal[None], w_s, 0)
    s = jnp.einsum('gts,bcsgd->bctgd', w, vb) + b_s.T[None, None, :, :, None]
    return u * s.reshape(B, T, SG_WIDTH)

def compress_blocks(k, pos, w1, b1, w2, b2):
    B, T, H, d = k.shape
    kc = k.reshape(B, T // CMP_STRIDE, CMP_STRIDE, H, d)
    blocks = jnp.concatenate([kc[:, :-1], kc[:, 1:]], axis=2) + pos[None, None, :, None, :]
    flat = blocks.transpose(0, 1, 3, 2, 4).reshape(B, -1, H, CMP_BLOCK * d)
    h = jax.nn.gelu(flat @ w1 + b1)
    return h @ w2 + b2

def nsa_attention(q, kv, gate_logits, q_norm_g, k_norm_g, cmp_pos, cmp_w1, cmp_b1, cmp_w2, cmp_b2):
    B, T = q.shape[:2]
    H, G, d = NSA_KV_HEADS, NSA_GROUP, HEAD_DIM
    n_cmp = T // CMP_STRIDE - 1
    n_slc = T // SLC_BLOCK
    n_sel = min(SLC_TOPK, n_slc)
    n_qb = T // Q_BLOCK
    scale = HEAD_DIM ** -0.5
    t_pos = jnp.arange(T)

    q = rms_norm_2(q.reshape(B, T, H, G, d), q_norm_g)
    k_cmp, v_cmp, k_slc, v_slc, k_win, v_win = [
        a.reshape(B, T, H, d) for a in jnp.split(kv, 6, axis=-1)]

    kc = rms_norm_2(compress_blocks(k_cmp, cmp_pos[0], cmp_w1[0], cmp_b1[0], cmp_w2[0], cmp_b2[0]), k_norm_g[0])
    vc = compress_blocks(v_cmp, cmp_pos[1], cmp_w1[1], cmp_b1[1], cmp_w2[1], cmp_b2[1])
    s_cmp = jnp.einsum('bthgd,bnhd->bhgtn', q, kc) * scale
    cmp_end = jnp.arange(n_cmp) * CMP_STRIDE + CMP_BLOCK - 1
    p_cmp = masked_softmax(s_cmp, cmp_end[None, :] <= t_pos[:, None])
    o_cmp = jnp.einsum('bhgtn,bnhd->bthgd', p_cmp.astype(vc.dtype), vc)

    cs = jnp.arange(n_cmp) * CMP_STRIDE
    ss = jnp.arange(n_slc) * SLC_BLOCK
    overlap = jnp.clip(jnp.minimum(cs[:, None] + CMP_BLOCK, ss[None, :] + SLC_BLOCK)
                       - jnp.maximum(cs[:, None], ss[None, :]), 0, None).astype(jnp.float32) / CMP_BLOCK
    imp = jnp.einsum('bhgtn,nj->bhtj', p_cmp, overlap)
    t_blk = t_pos[:, None] // SLC_BLOCK
    j = jnp.arange(n_slc)[None, :]
    forced = (j == 0) | (j == t_blk) | (j == t_blk - 1)
    imp = jnp.where(forced, FORCE_SCORE, jnp.where(j <= t_blk, imp, -FORCE_SCORE))
    _, sel = lax.top_k(imp, n_sel)

    k_slc = rms_norm_2(k_slc, k_norm_g[1])
    kb = k_slc.reshape(B, n_slc, SLC_BLOCK, H, d).transpose(0, 3, 1, 2, 4)
    vb = v_slc.reshape(B, n_slc, SLC_BLOCK, H, d).transpose(0, 3, 1, 2, 4)
    qb = q.reshape(B, n_qb, Q_BLOCK, H, G, d).transpose(1, 0, 2, 3, 4, 5)
    sb = sel.reshape(B, H, n_qb, Q_BLOCK, n_sel).transpose(2, 0, 1, 3, 4)
    tb = t_pos.reshape(n_qb, Q_BLOCK)
    bi = jnp.arange(B)[:, None, None, None]
    hi = jnp.arange(H)[None, :, None, None]

    def selected_block(args):
        qc, ic, tc = args
        kg = kb[bi, hi, ic].reshape(B, H, Q_BLOCK, n_sel * SLC_BLOCK, d)
        vg = vb[bi, hi, ic].reshape(B, H, Q_BLOCK, n_sel * SLC_BLOCK, d)
        key_pos = (ic[..., None] * SLC_BLOCK + jnp.arange(SLC_BLOCK)).reshape(B, H, Q_BLOCK, n_sel * SLC_BLOCK)
        mask = (key_pos <= tc[None, None, :, None])[:, :, None]
        s = jnp.einsum('bthgd,bhtmd->bhgtm', qc, kg) * scale
        p = masked_softmax(s, mask)
        return jnp.einsum('bhgtm,bhtmd->bthgd', p.astype(vg.dtype), vg)

    o_slc = lax.map(selected_block, (qb, sb, tb)).transpose(1, 0, 2, 3, 4, 5).reshape(B, T, H, G, d)

    k_win = rms_norm_2(k_win, k_norm_g[2])
    pad = ((0, 0), (WINDOW, 0), (0, 0), (0, 0))
    kp = jnp.pad(k_win, pad)
    vp = jnp.pad(v_win, pad)
    win_idx = jnp.arange(n_qb)[:, None] * Q_BLOCK + jnp.arange(WINDOW + Q_BLOCK)[None, :]
    kw = kp[:, win_idx]
    vw = vp[:, win_idx]
    qw = q.reshape(B, n_qb, Q_BLOCK, H, G, d)
    s_win = jnp.einsum('bcthgd,bckhd->bhgctk', qw, kw) * scale
    q_abs = tb[:, :, None]
    k_abs = (win_idx - WINDOW)[:, None, :]
    win_mask = (k_abs <= q_abs) & (k_abs > q_abs - WINDOW) & (k_abs >= 0)
    p_win = masked_softmax(s_win, win_mask)
    o_win = jnp.einsum('bhgctk,bckhd->bcthgd', p_win.astype(vw.dtype), vw).reshape(B, T, H, G, d)

    g = jax.nn.sigmoid(gate_logits.astype(jnp.float32)).reshape(B, T, H, G, N_BRANCH).astype(q.dtype)
    o = g[..., 0:1] * o_cmp + g[..., 1:2] * o_slc + g[..., 2:3] * o_win
    return o.reshape(B, T, NSA_WIDTH)

def memory_cross_attention_2(h, mem, kv_norm_g, w_mq, w_mkv, q_g, k_g, w_mo):
    B, T, _ = h.shape
    M = mem.shape[1]
    q = rms_norm_2((h @ w_mq).reshape(B, T, MEM_HEADS, MEM_HEAD_DIM), q_g)
    k, v = jnp.split(rms_norm_2(mem, kv_norm_g) @ w_mkv, 2, axis=-1)
    k = rms_norm_2(k.reshape(B, M, MEM_HEADS, MEM_HEAD_DIM), k_g)
    v = v.reshape(B, M, MEM_HEADS, MEM_HEAD_DIM)
    s = jnp.einsum('bthd,bmhd->bhtm', q, k) * MEM_HEAD_DIM ** -0.5
    p = jax.nn.softmax(s.astype(jnp.float32), axis=-1).astype(v.dtype)
    o = jnp.einsum('bhtm,bmhd->bthd', p, v).reshape(B, T, MEM_HEADS * MEM_HEAD_DIM)
    return o @ w_mo

def second_inputs(seed: int = 0) -> dict:
    key = jax.random.key(seed)
    ks = jax.random.split(key, 32)

    def nrm(k, shape, scale):
        return jax.random.normal(k, shape, jnp.float32) * scale

    def gain(k, shape):
        return 1.0 + 0.05 * jax.random.normal(k, shape, jnp.float32)

    L = DEPTH_2
    return {
        'x': nrm(ks[0], (BATCH, SEQ, D_MODEL), 1.0),
        'mem': nrm(ks[1], (BATCH, MEM_LEN, D_MODEL), 1.0),
        'norm_mix_g': gain(ks[2], (L, D_MODEL)),
        'w_in': nrm(ks[3], (L, D_MODEL, IN_COLS), D_MODEL ** -0.5),
        'sg_ln_g': gain(ks[4], (L, SG_WIDTH)),
        'sg_ln_b': nrm(ks[5], (L, SG_WIDTH), 0.02),
        'sg_w': nrm(ks[6], (L, SG_GROUPS, SG_CHUNK, SG_CHUNK), SG_CHUNK ** -0.5),
        'sg_b': 1.0 + nrm(ks[7], (L, SG_GROUPS, SG_CHUNK), 0.1),
        'q_norm_g': gain(ks[8], (L, HEAD_DIM)),
        'k_norm_g': gain(ks[9], (L, N_BRANCH, HEAD_DIM)),
        'cmp_pos': nrm(ks[10], (L, 2, CMP_BLOCK, HEAD_DIM), 0.5),
        'cmp_w1': nrm(ks[11], (L, 2, CMP_BLOCK * HEAD_DIM, CMP_HIDDEN), (CMP_BLOCK * HEAD_DIM) ** -0.5),
        'cmp_b1': nrm(ks[12], (L, 2, CMP_HIDDEN), 0.02),
        'cmp_w2': nrm(ks[13], (L, 2, CMP_HIDDEN, HEAD_DIM), CMP_HIDDEN ** -0.5),
        'cmp_b2': nrm(ks[14], (L, 2, HEAD_DIM), 0.02),
        'mix_out_g': gain(ks[15], (L, 2, SG_WIDTH)),
        'w_out': nrm(ks[16], (L, D_MIX, D_MODEL), D_MIX ** -0.5),
        'norm_mem_g': gain(ks[17], (L, D_MODEL)),
        'mem_kv_norm_g': gain(ks[18], (L, D_MODEL)),
        'w_mq': nrm(ks[19], (L, D_MODEL, MEM_HEADS * MEM_HEAD_DIM), D_MODEL ** -0.5),
        'w_mkv': nrm(ks[20], (L, D_MODEL, 2 * MEM_HEADS * MEM_HEAD_DIM), D_MODEL ** -0.5),
        'mem_q_norm_g': gain(ks[21], (L, MEM_HEAD_DIM)),
        'mem_k_norm_g': gain(ks[22], (L, MEM_HEAD_DIM)),
        'w_mo': nrm(ks[23], (L, MEM_HEADS * MEM_HEAD_DIM, D_MODEL), (MEM_HEADS * MEM_HEAD_DIM) ** -0.5),
        'norm_ffn_g': gain(ks[24], (L, D_MODEL)),
        'w_ff1': nrm(ks[25], (L, D_MODEL, D_FF_2), D_MODEL ** -0.5),
        'w_ff2': nrm(ks[26], (L, D_FF_2, D_MODEL), D_FF_2 ** -0.5),
    }

def second_block(x, mem, norm_mix_g, w_in, sg_ln_g, sg_ln_b, sg_w, sg_b, q_norm_g, k_norm_g,
              cmp_pos, cmp_w1, cmp_b1, cmp_w2, cmp_b2, mix_out_g, w_out,
              norm_mem_g, mem_kv_norm_g, w_mq, w_mkv, mem_q_norm_g, mem_k_norm_g, w_mo,
              norm_ffn_g, w_ff1, w_ff2):
    splits = [SG_WIDTH, 2 * SG_WIDTH, 2 * SG_WIDTH + NSA_WIDTH,
              2 * SG_WIDTH + NSA_WIDTH + 6 * KV_WIDTH]
    for l in range(DEPTH_2):
        h = rms_norm_2(x, norm_mix_g[l])
        z = h @ w_in[l]
        u, v, q, kv, gl = jnp.split(z, splits, axis=-1)
        a = spatial_gating_unit(jax.nn.gelu(u), jax.nn.gelu(v), sg_ln_g[l], sg_ln_b[l], sg_w[l], sg_b[l])
        b = nsa_attention(q, kv, gl, q_norm_g[l], k_norm_g[l], cmp_pos[l], cmp_w1[l], cmp_b1[l],
                          cmp_w2[l], cmp_b2[l])
        mixed = jnp.concatenate([rms_norm_2(a, mix_out_g[l, 0]), rms_norm_2(b, mix_out_g[l, 1])], axis=-1)
        x = x + mixed @ w_out[l]
        x = x + memory_cross_attention_2(rms_norm_2(x, norm_mem_g[l]), mem, mem_kv_norm_g[l], w_mq[l],
                                       w_mkv[l], mem_q_norm_g[l], mem_k_norm_g[l], w_mo[l])
        h = rms_norm_2(x, norm_ffn_g[l])
        x = x + jnp.square(jax.nn.relu(h @ w_ff1[l])) @ w_ff2[l]
    return x


def setup_inputs(seed=0):
    out = dict(first_inputs(seed))
    for name, value in second_inputs(seed + 1).items():
        if name != "x":
            out[name + "_2"] = value
    return out


def reference(
    x, mem, positions, rel_bias, w_in, q_norm_g, w_uq, kv_norm_g, w_ukv, w_mix_out, pre_mix_g,
    post_mix_g, w_xq, w_xk, w_xv, w_xo, mem_g, pre_xattn_g, post_xattn_g, w_up, w_down,
    pre_mlp_g, post_mlp_g, mem_2, norm_mix_g_2, w_in_2, sg_ln_g_2, sg_ln_b_2, sg_w_2, sg_b_2,
    q_norm_g_2, k_norm_g_2, cmp_pos_2, cmp_w1_2, cmp_b1_2, cmp_w2_2, cmp_b2_2, mix_out_g_2,
    w_out_2, norm_mem_g_2, mem_kv_norm_g_2, w_mq_2, w_mkv_2, mem_q_norm_g_2, mem_k_norm_g_2,
    w_mo_2, norm_ffn_g_2, w_ff1_2, w_ff2_2,
):
    x = first_block(
        x, mem, positions, rel_bias, w_in, q_norm_g, w_uq, kv_norm_g, w_ukv, w_mix_out,
        pre_mix_g, post_mix_g, w_xq, w_xk, w_xv, w_xo, mem_g, pre_xattn_g, post_xattn_g, w_up,
        w_down, pre_mlp_g, post_mlp_g,
    )
    return second_block(
        x, mem_2, norm_mix_g_2, w_in_2, sg_ln_g_2, sg_ln_b_2, sg_w_2, sg_b_2, q_norm_g_2,
        k_norm_g_2, cmp_pos_2, cmp_w1_2, cmp_b1_2, cmp_w2_2, cmp_b2_2, mix_out_g_2, w_out_2,
        norm_mem_g_2, mem_kv_norm_g_2, w_mq_2, w_mkv_2, mem_q_norm_g_2, mem_k_norm_g_2, w_mo_2,
        norm_ffn_g_2, w_ff1_2, w_ff2_2,
    )


_drawn_inputs = setup_inputs


def setup_inputs(seed=0):
    import zlib

    import numpy as np

    out = dict(_drawn_inputs(seed))
    spreads = {}
    factors = {'norm_mix_g_2': 2.695,
     'sg_ln_g_2': 8.0,
     'sg_ln_b_2': 8.0,
     'sg_b_2': 2.82,
     'q_norm_g_2': 8.0,
     'k_norm_g_2': 8.0,
     'cmp_b1_2': 8.0,
     'cmp_b2_2': 8.0,
     'mix_out_g_2': 3.217,
     'norm_mem_g_2': 8.0,
     'mem_kv_norm_g_2': 8.0,
     'mem_q_norm_g_2': 8.0,
     'mem_k_norm_g_2': 8.0,
     'norm_ffn_g_2': 7.173}
    for name, (base, spread) in spreads.items():
        noise = np.random.default_rng([zlib.crc32(name.encode()), seed]).standard_normal(out[name].shape)
        drawn = base * np.exp(spread * noise) if base else spread * noise
        out[name] = __import__('jax').numpy.asarray(drawn.astype(out[name].dtype))
    for name, factor in factors.items():
        out[name] = (out[name] * factor).astype(out[name].dtype)
    return out
```

```python
from contextlib import ExitStack

import numpy as np

import concourse.bass as bass
from concourse import mybir

F32 = mybir.dt.float32
F32R = mybir.dt.float32r
I32 = mybir.dt.int32
ALU = mybir.AluOpType
ACT = mybir.ActivationFunctionType
AX = mybir.AxisListType

P = 128
T = 256
TI = T // P
D = 1024
KD = D // P
EPS = 1e-6
DEPTH = 2
SLAB = 8 * 256
RAW = 2
RING = 3
P_RING, PT_RING = 4, 2
N_BANKS = 8
NEG = -1.0e30

Q_RANK, KV_RANK, ROPE = 384, 256, 32
HEADS = 8
MLA_SCALE = 96 ** -0.5
DIL_SCALE = 64 ** -0.5
X_SCALE = 256 ** -0.5
D_FF = 4096

G_PRE_MIX, G_POST_MIX, G_MEM, G_PRE_X, G_POST_X, G_PRE_MLP, G_POST_MLP, G_Q, G_KV = (
    0, 8, 16, 24, 32, 40, 48, 56, 59)
G_ROWS = 61
G_PITCH = 64

C_IDENT, C_SEL, C_BLOCK, C_CAUSAL = 0, 128, 256, 384
C_ONEHOT = 640
C_COL = 1152
C_CMP = 1160
C_PART = 1224
C_END = 1228


def shape_constants():
    c = np.zeros((P, C_END), np.float32)
    p = np.arange(P)
    c[:, C_IDENT:C_IDENT + P] = np.eye(P)
    for m in range(64, P):
        for r in (64 + m % 32, 96 + m % 32):
            c[r, C_SEL + m] = 1.0
    c[:, C_BLOCK:C_BLOCK + P] = (p[:, None] // 64 == p[None, :] // 64)
    key = np.arange(T)
    c[:, C_CAUSAL:C_CAUSAL + T] = np.where(key[None, :] - P <= p[:, None], 0.0, NEG)
    d = 255 - np.arange(512)
    near = np.maximum(d, 0)
    large = 16 + (np.log(np.maximum(near, 1).astype(np.float32) / np.float32(16))
                  / np.float32(np.log(128.0)) * np.float32(16)).astype(np.int32)
    bucket = np.where(near < 16, near, np.minimum(large, 31))
    times = ((d >= 0) & (d <= 128)) * 1.0 + ((d >= 0) & (d % 4 == 0)) + ((d >= 0) & (d % 16 == 0))
    lnm = np.where(times > 0, np.log(np.maximum(times, 1.0)), NEG)
    for b in range(32):
        c[b, C_ONEHOT:C_ONEHOT + 512] = bucket == b
    c[32, C_ONEHOT:C_ONEHOT + 512] = lnm
    inv = (np.float32(10000.0) ** (-np.arange(16, dtype=np.float32) / np.float32(16))).astype(np.float32)
    c[:, C_COL] = inv[p % 16]
    cos, sin = (p >= 64) & (p < 96), p >= 96
    c[:, C_COL + 1] = np.where(cos, -1.0, 0.0)
    c[:, C_COL + 2] = np.where(sin, np.where(p < 112, -1.0, 1.0), 0.0)
    c[:, C_COL + 3] = np.where(sin, 0.0, np.pi / 2)
    c[:, C_COL + 4] = EPS
    c[:, C_COL + 5] = 64 * EPS
    c[:, C_COL + 6] = 128 * EPS
    c[:, C_COL + 7] = 4 * EPS
    c[:, C_PART:C_PART + 4] = p[:, None] // 32 == np.arange(4)[None, :]
    for i in range(TI):
        t = i * P + p
        n = np.arange(32)
        c[:, C_CMP + 32 * i:C_CMP + 32 * i + 32] = np.where(
            (n[None, :] < 15) & (16 * n[None, :] + 31 <= t[:, None]), 0.0, NEG)
    return c


N_MIX, N_MEM, N_KV, N_FFN, N_B1, N_MQ, N_MK, N_SGB, N_Q, N_K, N_B2, N_POS, N_ROWS = (
    0, 8, 16, 24, 32, 36, 37, 38, 46, 47, 50, 52, 84)
N_CMP = 15
GELU_A, GELU_B = 0.044715, (2 / np.pi) ** 0.5

PER = {
    "slab_used": 64, "stat_mm": 7, "kpe_mm": 1, "scores": 16, "p_turned": 16, "pv": 16, "o_turned": 8,
    "first_bank": 5,
    "sumsq": 12,
    "slab_hi": 64, "act_hi": 32, "square": 24, "root": 7, "c_square": 1, "c_hi": 5, "kpe": 1,
    "v_evac": 6, "probs": 16, "pt_a": 8, "xkv_evac": 8, "o_hi": 8, "a_evac": 12, "h_sq": 16,
    "slab_lo": 64, "act_lo": 32, "rstd": 7, "gains": 1, "g_next": 1, "rope_k": 1, "z_evac": 20, "c_norm": 2,
    "c_lo": 5, "biased": 12, "neg_max": 16, "pt_v": 8, "o_evac": 8, "rinv": 8, "o_lo": 8,
    "x_part": 12, "x_new": 24, "up_scaled": 16, "h_lo": 16,
}
CREDIT = ["slab_lo", "root", "a_evac", "up_scaled", "x_new"]


TE_ORDER = (
    [("pair", 0), ("stat", 0), ("slab", 2), ("slab", 3), ("slab", 4), ("slab", 5), ("stat", 1),
     ("slab", 6), ("kpe", 0), ("slab", 7)] + [("scores", u) for u in range(4)] + [("slab", 8), ("slab", 9),
     ("turn", 0), ("scores", 4), ("turn", 1), ("pv", 0), ("scores", 5), ("turn", 2), ("pv", 1), ("slab", 10),
     ("turn", 3), ("pv", 2), ("turn", 4), ("pv", 3), ("slab", 11), ("turn", 5), ("pv", 4), ("pv", 5)]
    + [("scores", u) for u in range(6, 10)] + [("slab", 12), ("ot", 0), ("ot", 1), ("slab", 13), ("slab", 14),
     ("slab", 15), ("turn", 6), ("scores", 10), ("turn", 7), ("pv", 6), ("scores", 11), ("turn", 8), ("pv", 7),
     ("slab", 16), ("turn", 9), ("pv", 8), ("turn", 10), ("pv", 9), ("slab", 17), ("turn", 11), ("pv", 10),
     ("pv", 11), ("slab", 18), ("ot", 2), ("ot", 3), ("slab", 19)]
    + [("slab", s) for s in range(20, 24)] + [("stat", 2), ("pair", 24), ("stat", 3), ("slab", 26),
     ("slab", 27)] + [("scores", u) for u in range(12, 16)] + [("turn", 12), ("turn", 13), ("pv", 12),
     ("turn", 14), ("pv", 13), ("turn", 15), ("pv", 14), ("pv", 15)] + [("ot", b) for b in range(4, 8)]
    + [("slab", s) for s in range(28, 32)] + [("stat", 4), ("pair", 32), ("stat", 5)]
    + [("slab", s) for s in range(34, 64)] + [("stat", 6)])


TE_ORDER_2 = (
    [("pair", 0), ("stat", 0), ("slab", 2), ("slab", 3), ("slab", 4), ("hs", 0), ("sgw", 0), ("sgw", 1),
     ("slab", 5), ("slab", 6), ("hs", 1), ("hs", 2), ("slab", 7), ("slab", 8), ("slab", 9), ("hs", 3), ("slab", 10)]
    + [("scores", u) for u in range(4)] + [("slab", 11), ("slab", 12), ("turn", 0), ("scores", 4), ("turn", 1),
     ("pv", 0), ("scores", 5), ("turn", 2), ("pv", 1), ("slab", 13), ("turn", 3), ("pv", 2), ("turn", 4), ("pv", 3),
     ("slab", 14), ("turn", 5), ("pv", 4), ("pv", 5)]
    + [("vturn", 0), ("cscores", 0), ("cscores", 1)] + [("mem", b) for b in range(4)]
    + [("scores", u) for u in range(6, 10)] + [("slab", 15), ("sgu", 0), ("sgu", 1), ("slab", 16), ("hs", 4), ("hs", 5),
     ("cturn", 0), ("cpv", 0), ("cpv", 1), ("turn", 6), ("scores", 10), ("turn", 7), ("pv", 6), ("scores", 11),
     ("turn", 8), ("pv", 7), ("slab", 17), ("turn", 9), ("pv", 8), ("turn", 10), ("pv", 9), ("turn", 11), ("pv", 10),
     ("pv", 11), ("slab", 18)] + [("ot", b) for b in range(4)]
    + [("slab", s) for s in range(19, 23)] + [("pair", 23), ("stat", 1), ("hs", 6), ("hs", 7)]
    + [("scores", u) for u in range(12, 16)] + [("turn", 12), ("turn", 13), ("pv", 12), ("turn", 14), ("pv", 13),
     ("turn", 15), ("pv", 14), ("pv", 15)] + [("ot", 4), ("ot", 5)]
    + [("slab", 25), ("slab", 26), ("pair", 27), ("stat", 2)] + [("slab", s) for s in range(29, 51)]
    + [("out", 0)] + [("slab", s) for s in range(51, 55)] + [("out", 1)] + [("slab", s) for s in range(55, 59)]
    + [("out", 2), ("out", 3)])


def slab_banks_2(s):
    if s < 5:
        return [(f"y{s}", "y_evac", s + 1)]
    if s in (5, 7):
        return [(f"ch{(s - 5) // 2}", "ch_evac", (s - 5) // 2 + 1)]
    if s in (6, 8):
        return []
    if s == 9:
        return [("kc", "kc_evac", 3)]
    if s == 10:
        return [("gates", "gate_exp", 1)]
    if s < 15:
        return [(f"g{s - 11}", "g_evac", s - 10)]
    if s < 17:
        return [(f"mk{s - 15}", "mk_evac", s - 14)]
    if s < 19:
        return [(f"mv{s - 17}", "mv_evac", s - 16)]
    if s < 23:
        return [(f"w{s - 19}", "w_evac", s - 18)]
    if s < 25:
        return [(f"mq{s - 23}", "mq_evac", s - 22)]
    if s < 27:
        return [(f"mo{b}", "w_evac", 5 + b) for b in (2 * (s - 25), 2 * (s - 25) + 1)]
    if s < 43:
        return [(f"up{s - 27}", "up_scaled", s - 26)]
    b, c = divmod(s - 43, 4)
    return [(f"down{b}", "w_evac", 9 + b)] if c == 0 else []


def bank_uses_2():
    uses = []
    for kind, n in TE_ORDER_2:
        if kind == "slab":
            uses += slab_banks_2(n)
        elif kind == "pair":
            uses += slab_banks_2(n) + slab_banks_2(n + 1)
        elif kind == "scores":
            uses.append((f"scores{n}", "biased" if n < 12 else "probs", n + 1))
        elif kind == "turn":
            uses.append((f"turn{n}", *pt_signal(n)))
        elif kind == "pv":
            b, opens, _ = o_bank_2(n)
            if opens:
                uses.append((f"o{b}", "o_evac", b + 1))
        elif kind == "cpv":
            uses.append((f"oc{n}", "b_part", n + 1))
        elif kind == "mem":
            uses.append((f"mem{n}", "act_lo", 10 + 2 * n))
        else:
            signal = {"stat": "root", "sgw": "sgw_evac", "hs": "hs_root", "vturn": "vblk",
                      "cscores": "c_biased", "sgu": "sgu_evac", "cturn": "cturn_evac", "ot": "o_lo", "out": "out_evac"}[kind]
            uses.append((f"{kind}{n}", signal, n + 1))
    return uses


def o_bank_2(u):
    if u < 12:
        return o_bank(u)
    return 4 + (u - 12) // 2, u % 2 == 0, u % 2 == 1


ONCE = [
    "hs_mm", "sgw_turned", "mem_turned", "vturned", "c_scores", "c_turned", "c_pv", "sgu_mm", "out_turned",
    "mem_scaled", "b_sum",
    "cin_hi", "mem_sum", "mem_root", "hs_square", "hs_root", "sgw_evac", "ch_tanh", "ch_hi", "gate_exp", "g_evac",
    "g_square", "g_tanh", "ln_var", "ln_root", "c_exp", "mv_evac", "ab_var", "ab_root", "out_evac",
    "step", "y_evac", "cin", "cin_lo", "sgw_masked", "mem_inv", "hs_rstd", "hs_done", "ch_evac", "ch_poly", "ch_g",
    "ch_lo", "kc_evac", "neg_rstd", "g_poly", "g_out", "ln_center", "ln_done", "vblk", "c_biased", "c_ready",
    "mk_evac", "sgu_evac", "sgu_out", "cturn_evac", "b_part", "ab_scaled", "w_evac", "mq_evac",
    "ln_loaded", "sgw_loaded", "mem_loaded", "out_gain_loaded",
]


def slab_banks(s):
    if s < 3:
        return [(f"z{s}", "z_evac", s + 1)]
    if s < 7:
        return [(f"z{s}", "z_evac", s + 2)]
    if s < 9:
        return [(f"z{s}", "v_evac", 2 * (s - 6))]
    if s < 11:
        return [(f"uq{b}", "z_evac", 9 + b) for b in (2 * (s - 9), 2 * (s - 9) + 1)]
    if s == 11:
        return [("uk0", "z_evac", 14), ("uk1", "z_evac", 16), ("uv0", "v_evac", 5), ("uv1", "v_evac", 6)]
    for first, name, signal, done in ((12, "xk", "xkv_evac", 1), (16, "xv", "xkv_evac", 5), (20, "mix", "a_evac", 1),
                                      (24, "xq", "z_evac", 17), (28, "xo", "a_evac", 5)):
        if s < first + 4:
            return [(f"{name}{s - first}", signal, done + s - first)]
    if s < 48:
        return [(f"up{s - 32}", "up_scaled", s - 31)]
    b, c = divmod(s - 48, 4)
    return [(f"down{b}", "a_evac", 9 + b)] if c == 0 else []


def bank_uses():
    uses = []
    for kind, n in TE_ORDER:
        if kind == "slab":
            uses += slab_banks(n)
        elif kind == "pair":
            uses += slab_banks(n) + slab_banks(n + 1)
        elif kind == "stat":
            uses.append((f"stat{n}", "root", n + 1))
        elif kind == "kpe":
            uses.append(("kpe", "kpe", 1))
        elif kind == "scores":
            uses.append((f"scores{n}", "biased", n + 1) if n < 12 else (f"scores{n}", "probs", n + 1))
        elif kind == "turn":
            uses.append((f"turn{n}", *pt_signal(n)))
        elif kind == "ot":
            uses.append((f"ot{n}", "o_lo", n + 1))
        elif o_bank(n)[1]:
            uses.append((f"o{o_bank(n)[0]}", "o_evac", o_bank(n)[0] + 1))
    return uses + [None] * (-len(uses) % N_BANKS)


def o_bank(u):
    if u < 12:
        return 2 * (u // 6) + (u % 6 > 1), u % 6 in (0, 2), u % 6 in (1, 5)
    return u - 8, True, True


def pt_signal(u):
    return ("pt_v" if u % 2 == 0 else "pt_a", u // 2 + 1)


def gain_rows_2(A):
    def rows(name):
        return A[name + "_2"][0].rearrange("(r c) -> r c", c=P)
    return [
        (N_MIX, rows("norm_mix_g")), (N_MEM, rows("norm_mem_g")), (N_KV, rows("mem_kv_norm_g")),
        (N_FFN, rows("norm_ffn_g")), (N_B1, A["cmp_b1_2"][0].rearrange("a (r c) -> (a r) c", c=P)),
        (N_MQ, rows("mem_q_norm_g")), (N_MK, rows("mem_k_norm_g")), (N_SGB, A["sg_b_2"][0]),
        (N_Q, A["q_norm_g_2"]), (N_K, A["k_norm_g_2"][0]), (N_B2, A["cmp_b2_2"][0]),
        (N_POS, A["cmp_pos_2"][0].rearrange("a (r e) c -> (a r) (e c)", e=2)),
    ]


def build(nc, A, out):
    ctx = ExitStack()
    with ctx:
        def sem(name):
            return ctx.enter_context(nc.semaphore(name))

        def sb(name, shape, dt=F32, on=ctx):
            return on.enter_context(nc.sbuf_tensor(name, shape, dt))

        raw = sb("raw", [P, RAW, SLAB])
        w_hi = sb("w_hi", [P, RING, SLAB], F32R)
        w_lo = sb("w_lo", [P, RING, SLAB], F32R)
        x_t = sb("x_t", [P, KD, T])
        act_hi = sb("act_hi", [P, KD, T], F32R)
        act_lo = sb("act_lo", [P, KD, T], F32R)
        mem_t = sb("mem_t", [P, KD, T])
        cst = sb("cst", [P, C_END])
        toep = sb("toep", [P, HEADS, T])
        rope = sb("rope", [P, T])
        rope_q = sb("rope_q", [P, T])
        rope_k = sb("rope_k", [P, T])
        g_all = sb("g_all", [P, DEPTH, G_PITCH])
        g_pre = sb("g_pre", [P, DEPTH + 1, 8])
        g_next = sb("g_next", [P, 8])
        g_cur = sb("g_cur", [P, G_PITCH])
        g_2 = sb("g_2", [P, N_ROWS])
        sumsq = sb("sumsq", [P, 2 * T])
        sq_next = sb("sq_next", [P, 2 * T])
        root = sb("root", [P, 2 * T])
        rstd = sb("rstd", [P, T + TI])
        rstd_c = sb("rstd_c", [P, 2, T])
        neg_max = sb("neg_max", [P, 48])
        row_sum = sb("row_sum", [P, 48])
        row_inv = sb("row_inv", [P, 48])
        small = sb("small", [P, 16])
        qk_dil = sb("qk_dil", [P, KD, T])
        probs = sb("probs", [P, P_RING, 512])
        p_t = sb("p_t", [P, PT_RING, 512])
        early = ExitStack()
        with early:
            q_t = sb("q_t", [P, HEADS, T], on=early)
            k_t = sb("k_t", [P, HEADS, T], on=early)
            v_mla = sb("v_mla", [P, TI, 512], on=early)
            v_dil = sb("v_dil", [P, TI, 512], on=early)
            o_tok = sb("o_tok", [P, TI, 512], on=early)
            o_hi = sb("o_hi", [P, KD, T], F32R, on=early)
            o_lo = sb("o_lo", [P, KD, T], F32R, on=early)
            kx_t = sb("kx_t", [P, KD, T], on=early)
            vx = sb("vx", [P, TI, D], on=early)
            head_sq = sb("head_sq", [P, 2, 512], on=early)
        h_hi = sb("h_hi", [P, 32, T], F32R)
        h_lo = sb("h_lo", [P, 32, T], F32R)

        banks = [ctx.enter_context(nc.psum_tensor(f"bank{b}", [P, 512], F32)) for b in range(N_BANKS)]
        toep_rows = nc.dram_tensor("toep_rows", [HEADS, 512], F32, kind="Internal").ap()
        toep_skew = nc.dram_tensor("toep_skew", [HEADS, P, 512], F32, kind="Internal").ap()

        sig = {name: sem(name) for name in PER}
        raw_loaded = [sem(f"raw_loaded{r}") for r in range(RAW)]
        i_load = {n: sem("i_" + n) for n in ("cst", "x", "mem", "gains", "pos", "relb", "rows", "skew", "toep", "gains_2",
                                         "ident", "first_gain")}
        i_clear = sem("i_clear")
        i_turned = sem("i_turned")
        i_evac = sem("i_evac")
        i_mem_evac = sem("i_mem_evac")
        i_stat = sem("i_stat")
        i_inv = sem("i_inv")
        i_scaled = sem("i_scaled")
        i_step = sem("i_step")
        i_arg = sem("i_arg")
        i_sin = sem("i_sin")
        i_tables = sem("i_tables")
        out_stored = sem("out_stored")
        once = {name: sem("b2_" + name) for name in ONCE}

        def value(name, layer, n):
            return layer * PER[name] + (n + (PER[name] if name in CREDIT else 0))

        ident = cst[:, C_IDENT:C_IDENT + P]
        sel = cst[:, C_SEL:C_SEL + P]
        ones = sb("ones", [P, P])
        causal = cst[:, C_CAUSAL:C_CAUSAL + T]
        eps = cst[:, C_COL + 4:C_COL + 5]

        def twice(ap):
            return ap.unsqueeze(1).broadcast_to([ap.shape[0], 2, T])

        def halves(bank):
            return bank.rearrange("p (a t) -> p a t", a=2)

        def slab_source(l, s):
            def cols(name, a, b, r0=0, r1=D):
                return A[name][l, r0:r1, a:b].rearrange("(k p) n -> p k n", p=P)
            w_in = [(0, 256), (256, 512), (672, 928), (512, 672), (928, 1184), (1184, 1440),
                    (1440, 1696), (1696, 1952), (1952, 2208)]
            if s < 9:
                return cols("w_in", *w_in[s])
            if s < 11:
                return cols("w_uq", 384 * (s - 9), 384 * (s - 8), 0, Q_RANK)
            if s == 11:
                return cols("w_ukv", 0, 1024, 0, KV_RANK)
            for first, name in ((12, "w_xk"), (16, "w_xv"), (20, "w_mix_out"), (24, "w_xq"), (28, "w_xo")):
                if s < first + 4:
                    return cols(name, 256 * (s - first), 256 * (s - first + 1))
            if s < 48:
                return cols("w_up", 256 * (s - 32), 256 * (s - 31))
            b, c = divmod(s - 48, 4)
            return cols("w_down", 256 * b, 256 * b + 256, D * c, D * (c + 1))

        def slab_pieces(s):
            if s == 3:
                d, r = (8, 256), (8, 160)
                return d, r, [((0, 128), (0, 128)), ((128, 224), (64, 160)),
                              ((224, 240), (144, 160)), ((240, 256), (128, 144))]
            if s in (9, 10):
                d, r = (12, 128), (12, 96)
                return d, r, [((0, 96), (0, 96)), ((96, 112), (80, 96)), ((112, 128), (64, 80))]
            return (1, SLAB), (1, SLAB), [((0, SLAB), (0, SLAB))]

        def slab_source_2(s):
            def cols(name, a, b, r0=0, r1=D):
                return A[name + "_2"][0, r0:r1, a:b].rearrange("(k p) n -> p k n", p=P)
            if s < 3:
                return cols("w_in", 1536 + 256 * s, 1792 + 256 * s)
            if s < 5:
                return A["w_in_2"][0, :, 1024:1536].rearrange("(k p) (v n) -> p k v n", p=P, v=2)[
                    :, :, :, P * (s - 3):P * (s - 2)]
            if s < 9:
                kind, half = divmod(s - 5, 2)
                return A["cmp_w1_2"][0, kind, D * half:D * half + D, :].rearrange("(k p) n -> p k n", p=P)
            if s == 9:
                return A["cmp_w2_2"][0].rearrange("a (k p) n -> p (a k) n", p=P)
            if s == 10:
                return cols("w_in", 2304, 2328)
            if s < 15:
                c = 256 * ((s - 9) % 4)
                return cols("w_in", c, c + 256)
            if s < 19:
                return cols("w_mkv", 256 * (s - 15), 256 * (s - 14))
            if s < 23:
                return cols("w_out", 256 * (s - 19), 256 * (s - 18))
            if s < 25:
                return cols("w_mq", 256 * (s - 23), 256 * (s - 22))
            if s < 27:
                return cols("w_mo", 512 * (s - 25), 512 * (s - 24), 0, 512)
            if s < 43:
                return cols("w_ff1", 256 * (s - 27), 256 * (s - 26))
            b, c = divmod(s - 43, 4)
            return cols("w_ff2", 256 * b, 256 * b + 256, D * c, D * (c + 1))

        def split_views_2(s, dst, src):
            if s in (3, 4):
                d = dst.rearrange("p (k m v c) -> p k m v c", k=8, m=2, v=2)
                r = src.rearrange("p (k v m c) -> p k m v c", k=8, v=2, m=2)
                return [(d[:, :, m], r[:, :, m]) for m in range(2)]
            if s == 9:
                d = dst[:, 0:512].rearrange("p (k a n) -> p k a n", k=4, a=2)
                r = src[:, 0:256].rearrange("p (k n) -> p k n", k=4)
                return [(d[:, :, a], r) for a in range(2)]
            n = 8 * 24 if s == 10 else SLAB
            return [(dst[:, 0:n], src[:, 0:n])]

        def split_views(s, dst, src):
            if s == 11:
                out = []
                for kind in range(2):
                    d = dst[:, 1024 * kind:1024 * kind + 1024].rearrange("p (k h c) -> p k h c", k=2, h=8)
                    r = src.rearrange("p (k h c) -> p k h c", k=2, h=8)[:, :, :, 64 * kind:64 * kind + 64]
                    for k in range(2):
                        out.append((d[:, k], r[:, k]))
                return out
            (da, db), (ra, rb), pieces = slab_pieces(s)
            d = dst[:, 0:da * db].rearrange("p (a b) -> p a b", a=da)
            r = src[:, 0:ra * rb].rearrange("p (a b) -> p a b", a=ra)
            return [(d[:, :, x0:x1], r[:, :, y0:y1]) for (x0, x1), (y0, y1) in pieces]

        def slot(layer, s):
            if second(layer) or s < 16:
                return s % RING
            return (s + 2) % RING

        def split_hi(act, layer, s):
            loads = s // RAW + 1 + (second(layer) and s >= 3)
            act.wait_ge(raw_loaded[s % RAW], layer * (16 * 32) + 16 * loads)
            if s >= 3:
                last = s - 2 if second(layer) else {16: 16, 17: 14, 18: 15}.get(s, s - 2)
                act.wait_ge(sig["slab_used"], value("slab_used", layer, last))
            pieces = split_views_2 if second(layer) else split_views
            views = pieces(s if s < 64 else 0, w_hi[:, slot(layer, s)], raw[:, s % RAW])
            for n, (d, r) in enumerate(views):
                ins = act.activation(d, r, ACT.Copy)
            ins.then_inc(sig["slab_hi"], 1)

        def split_lo(dve, layer, s):
            dve.wait_ge(sig["slab_hi"], value("slab_hi", layer, s + 1))
            sp = s if s < 64 else 0
            pieces = split_views_2 if second(layer) else split_views
            for (d, r), (h, _) in zip(pieces(sp, w_lo[:, slot(layer, s)], raw[:, s % RAW]),
                                      pieces(sp, w_hi[:, slot(layer, s)], raw[:, s % RAW])):
                ins = dve.tensor_tensor(d, r, h.bitcast(F32), ALU.subtract)
            ins.then_inc(sig["slab_lo"], 1)

        USES = bank_uses()
        NU = len(USES)
        INDEX = {u[0]: n for n, u in enumerate(USES) if u}

        USES_2 = bank_uses_2()
        INDEX_2 = {u[0]: n for n, u in enumerate(USES_2)}

        def second(layer):
            return isinstance(layer, int) and layer == DEPTH

        def bank(use, layer=0):
            return banks[(INDEX_2 if second(layer) else INDEX)[use] % N_BANKS]

        def open_bank(pe, layer, use):
            n = (INDEX_2 if second(layer) else INDEX)[use] - N_BANKS
            if second(layer) and n >= 0:
                _, name, count = USES_2[n]
                if name in once:
                    pe.wait_ge(once[name], count)
                else:
                    pe.wait_ge(sig[name], value(name, DEPTH, count))
                return bank(use, layer)
            while USES[n % NU] is None:
                n -= N_BANKS
            _, name, count = USES[n % NU]
            pe.wait_ge(sig[name], value(name, layer, count - (PER[name] if n < 0 else 0)))
            return bank(use, layer)

        def products3(pe, o, stat_hi, stat_lo, mov_hi, mov_lo, first, last):
            pe.matmul(o, stat_hi, mov_hi, start=first, stop=False)
            pe.matmul(o, stat_hi, mov_lo, start=False, stop=False)
            return pe.matmul(o, stat_lo, mov_hi, start=False, stop=last)

        def w_view(layer, s, cols):
            return (w_hi[:, slot(layer, s)].rearrange("p (k n) -> p k n", n=cols),
                    w_lo[:, slot(layer, s)].rearrange("p (k n) -> p k n", n=cols))

        def columns_slab(pe, layer, s, o, src_hi, src_lo, ready=None, first=True, last=True):
            pe.wait_ge(sig["slab_lo"], value("slab_lo", layer, s + 1))
            wh, wl = w_view(layer, s, 256)
            for m in range(2):
                c = slice(128 * m, 128 * m + 128)
                for k in range(8):
                    if ready is not None and m == 0:
                        ready(k)
                    ins = products3(pe, o[:, T * m:T * m + T], wh[:, k, c], wl[:, k, c],
                                    src_hi[:, k], src_lo[:, k], first and k == 0, last and k == 7)
            ins.then_inc(sig["slab_used"], 1)

        def slab_pair(pe, layer, s, names, ready):
            outs = [open_bank(pe, layer, name) for name in names]
            for n in range(2):
                pe.wait_ge(sig["slab_lo"], value("slab_lo", layer, s + n + 1))
            for k in range(8):
                pe.wait_ge(sig["act_lo"], value("act_lo", layer, ready + k + 1))
                for n, o in enumerate(outs):
                    wh, wl = w_view(layer, s + n, 256)
                    if second(layer) and s + n == 1:
                        tiles = [(o[:, 0:T], wh[:, k, 0:P], wl[:, k, 0:P], act_hi[:, k], act_lo[:, k])]
                        for i in range(TI):
                            t = slice(P * i, P * i + P)
                            tiles.append((o[:, T + P * i:T + P * i + P], act_hi[:, k, t], act_lo[:, k, t],
                                          wh[:, k, P:2 * P], wl[:, k, P:2 * P]))
                    else:
                        tiles = [(o[:, T * m:T * m + T], wh[:, k, P * m:P * m + P], wl[:, k, P * m:P * m + P],
                                  act_hi[:, k], act_lo[:, k]) for m in range(2)]
                    for m, (dst, stat_hi, stat_lo, mov_hi, mov_lo) in enumerate(tiles):
                        pe.matmul(dst, stat_hi, mov_hi, start=k == 0 and m == 0, stop=False, skip_group_check=True)
                        pe.matmul(dst, stat_hi, mov_lo, start=False, stop=False, skip_group_check=True)
                        ins = pe.matmul(dst, stat_lo, mov_hi, start=False, stop=k == 7, skip_group_check=True)
                    if k == 7:
                        ins.then_inc(sig["slab_used"], 1)

        def rows_slab(pe, layer, s, o, src_hi, src_lo):
            pe.wait_ge(sig["slab_lo"], value("slab_lo", layer, s + 1))
            wh, wl = w_view(layer, s, 256)
            for i in range(TI):
                t = slice(P * i, P * i + P)
                for k in range(8):
                    ins = products3(pe, o[:, T * i:T * i + T], src_hi[:, k, t], src_lo[:, k, t],
                                    wh[:, k], wl[:, k], k == 0, k == 7)
            ins.then_inc(sig["slab_used"], 1)

        def unit(u):
            if u < 2:
                return 0, range(u, HEADS, 2), 1
            first = 4 * (u % 2) + u // 4
            return 1, range(first, first + 4, 2), 2

        def unit_2(u):
            if u < 2:
                return 0, range(4 * u, 4 * u + 4), 1
            return 1, range(2 * u - 4, 2 * u - 2), 2

        def x_unit(u):
            return u // 2, (2 * (u % 2), 2 * (u % 2) + 1)

        latents = vx[:, :, :].rearrange("p i n -> p (i n)").rearrange("p (k t) -> p k t", t=T)

        def flat(tile):
            return tile[:, :, :].rearrange("p a b -> p (a b)")

        def v2(name, n):
            return value(name, DEPTH, n)

        k_pairs = k_t[:, 2:6, :]
        out_gain = flat(k_t)[:, 512:1536].rearrange("p (b n) -> p b n", b=2)
        gelu_part = [k_t[:, 6:8, :], v_mla[:, :, 256:512]]
        cin = flat(o_tok)[:, 0:32 * 30]
        cin_hi, cin_lo = flat(o_hi)[:, 0:32 * 30], flat(o_lo)[:, 0:32 * 30]
        ch_hi, ch_lo = flat(o_hi)[:, 960:1080], flat(o_lo)[:, 960:1080]
        ch_x, ch_y, ch_z = rope[:, 0:120], rope_q[:, 0:120], rope_k[:, 0:120]
        ln_rows = flat(toep)[:, 0:1024].rearrange("p (b n) -> p b n", b=2)
        sg_w = flat(toep)[:, 1024:2048].rearrange("p (g s) -> p g s", g=8)
        mem_rows_2 = flat(kx_t).rearrange("p (i n) -> p i n", i=TI)
        mem_v = flat(kx_t)[:, 1024:2048].rearrange("p (i n) -> p i n", i=TI)
        b_tok = flat(q_t)[:, 1024:2048].rearrange("p (i n) -> p i n", i=TI)
        a_tok = vx[:, :, 512:1024]
        gates = rope[:, 128:176].rearrange("p (i h b) -> p i h b", i=TI, b=3)
        coef = rope[:, 176:224].rearrange("p (b i h) -> p b i h", b=3, i=TI)
        c_max, c_sum = rope_q[:, 128:144], rope_q[:, 144:160]
        ln_stat, mem_stat = rope_q[:, 176:182], rope_q[:, 182:186]
        ab_stat, neg_rstd = rope_q[:, 186:190], rope_q[:, 190:192]
        c_p = flat(qk_dil)[:, 0:512].rearrange("p (v a) -> p v a", v=2)
        c_pt = flat(qk_dil)[:, 512:1024].rearrange("p (v i t) -> p v i t", v=2, i=TI)
        c_z = flat(qk_dil)[:, 1024:1280].rearrange("p (v a) -> p v a", v=2)
        c_v = flat(qk_dil)[:, 1280:1792].rearrange("p (v a) -> p v a", v=2)
        kc = flat(qk_dil)[:, 1792:1856].rearrange("p (v n) -> p v n", v=2)
        kc_raw = flat(qk_dil)[:, 1856:1886]
        out_rows = flat(qk_dil).rearrange("p (b i n) -> p b i n", b=4, i=TI)

        prologue_x = flat(q_t).rearrange("p (i n) -> p i n", i=TI)
        prologue_mem = flat(k_t).rearrange("p (i n) -> p i n", i=TI)

        block = ctx.enter_context(nc.Block())

        @block.sync
        def _(sp):
            for name in CREDIT:
                sp.sem_inc(sig[name], PER[name])
            sp.dma_start(ident, A["shape_constants"][:, C_IDENT:C_IDENT + P]).then_inc(i_load["ident"], 16)
            sp.dma_start(q_t[:, :, :].rearrange("p a b -> p (a b)").rearrange("p (i n) -> p i n", i=TI),
                         A["x"][0].rearrange("(i p) n -> p i n", p=P)).then_inc(i_load["x"], 16)
            sp.dma_start(k_t[:, :, :].rearrange("p a b -> p (a b)").rearrange("p (i n) -> p i n", i=TI),
                         A["mem"][0].rearrange("(i p) n -> p i n", p=P)).then_inc(i_load["mem"], 16)

            def load(layer, s):
                sp.wait_ge(sig["slab_lo"], value("slab_lo", layer, s - RAW + 1))
                src = slab_source(layer, s)
                a, b = src.shape[1], src.shape[2]
                sp.dma_start(raw[:, s % RAW, 0:a * b].rearrange("p (k n) -> p k n", k=a), src)\
                    .then_inc(raw_loaded[s % RAW], 16)

            with sp.Fori(0, DEPTH) as layer:
                for s in range(64):
                    load(layer, s)
            for s in range(59):
                sp.wait_ge(sig["slab_lo"], v2("slab_lo", s - RAW + 1))
                src = slab_source_2(s)
                n = int(np.prod(src.shape[1:]))
                dst = raw[:, s % RAW, 0:n]
                if s in (3, 4):
                    dst = dst.rearrange("p (k v n) -> p k v n", k=8, v=2)
                    for v in range(2):
                        sp.dma_start(dst[:, :, v], src[:, :, v]).then_inc(raw_loaded[s % RAW], 16)
                else:
                    sp.dma_start(dst.rearrange("p (k n) -> p k n", k=src.shape[1]), src)\
                        .then_inc(raw_loaded[s % RAW], 16)
            for b in range(4):
                sp.wait_ge(once["out_evac"], b + 1)
                sp.dma_start(out[0, :, 256 * b:256 * b + 256].rearrange("(i p) n -> p i n", p=P), out_rows[:, b])\
                    .then_inc(out_stored, 16)
            sp.wait_ge(out_stored, 16 * 4)

        @block.gpsimd
        def _(pool):
            def add_squares(layer, norm):
                for j in range(1, 3):
                    pool.wait_ge(sig["square"], value("square", layer, 4 * norm + j + 1))
                    pool.tensor_tensor(sumsq[:, :], sumsq[:, :], sq_next[:, :], ALU.add)\
                        .then_inc(sig["sumsq"], 1)

            pool.memset(v_mla[:, 0, 0:2 * P], 0.0).then_inc(i_clear, 1)
            pool.memset(small[0:33, 0:8], 1.0).then_inc(i_clear, 1)
            pool.memset(ones[:, :], 1.0).then_inc(i_clear, 1)
            pool.memset(v_mla[:, 1, 0:P], 0.0).then_inc(i_clear, 1)
            pool.memset(v_mla[:, 1, P:3 * P], 0.0).then_inc(i_clear, 1)
            pool.wait_ge(i_clear, 5)
            pool.dma_start(vx[:, 0, 0:T].bitcast(I32), bass.AP(A["positions"].tensor, 0, [[0, P], [1, T]]))\
                .then_inc(i_load["pos"], 16)
            pool.dma_start(v_mla[0:8, 1, P:3 * P].rearrange("r (l c) -> r l c", l=DEPTH),
                           A["pre_mix_g"].rearrange("l (r c) -> r l c", c=P)).then_inc(i_load["first_gain"], 16)
            pool.dma_start(small[0:32, 0:8], A["rel_bias"]).then_inc(i_load["relb"], 16)
            for name, row in (("pre_mix_g", G_PRE_MIX), ("post_mix_g", G_POST_MIX), ("mem_g", G_MEM),
                              ("pre_xattn_g", G_PRE_X), ("post_xattn_g", G_POST_X),
                              ("pre_mlp_g", G_PRE_MLP), ("post_mlp_g", G_POST_MLP),
                              ("q_norm_g", G_Q), ("kv_norm_g", G_KV)):
                n = A[name].shape[1] // P
                pool.dma_start(v_mla[row:row + n, 0, 0:2 * P].rearrange("r (l c) -> r l c", l=DEPTH),
                               A[name].rearrange("l (r c) -> r l c", c=P)).then_inc(i_load["gains"], 16)
            add_squares(0, 0)
            pool.wait_ge(i_evac, 7)
            pool.dma_start(toep_rows, qk_dil[0:HEADS, 0:2, :].rearrange("h a b -> h (a b)"))\
                .then_inc(i_load["rows"], 16)
            pool.wait_ge(i_load["rows"], 16)
            pool.dma_start(toep_skew, bass.AP(toep_rows.tensor, 0, [[512, HEADS], [0, P], [1, 512]]))\
                .then_inc(i_load["skew"], 16)
            pool.wait_ge(i_load["skew"], 16)
            pool.dma_start(toep[:, :, :], bass.AP(toep_skew.tensor, P - 1, [[511, P], [P * 512, HEADS], [1, T]]))\
                .then_inc(i_load["toep"], 16)

            with pool.Fori(0, DEPTH) as layer:
                for norm in range(1, 7):
                    add_squares(layer, norm)
            pool.wait_ge(sig["biased"], value("biased", DEPTH - 1, 6))
            for b, name in enumerate(("sg_ln_g_2", "sg_ln_b_2")):
                pool.dma_start(ln_rows[:, b, :], bass.AP(A[name].tensor, 0, [[0, P], [1, 512]]))\
                    .then_inc(once["ln_loaded"], 16)
            pool.dma_start(sg_w, A["sg_w_2"][0].rearrange("g t s -> t g s")).then_inc(once["sgw_loaded"], 16)
            pool.wait_ge(sig["slab_used"], value("slab_used", DEPTH - 1, 64))
            pool.dma_start(mem_rows_2, A["mem_2"][0].rearrange("(i p) n -> p i n", p=P))\
                .then_inc(once["mem_loaded"], 16)
            pool.wait_ge(once["cin"], 1)
            pool.dma_start(out_gain, bass.AP(A["mix_out_g_2"].tensor, 0, [[0, P], [512, 2], [1, 512]]))\
                .then_inc(once["out_gain_loaded"], 16)
            pool.wait_ge(once["mem_inv"], 1)
            for i in range(TI):
                pool.tensor_scalar(mem_rows_2[:, i], mem_rows_2[:, i], mem_stat[:, 2 + i:3 + i], None, ALU.mult)\
                    .then_inc(once["mem_scaled"], 1)
            for n in range(4):
                if n < TI:
                    pool.wait_ge(once["b_part"], n + 1)
                    pool.wait_ge(sig["o_evac"], v2("o_evac", n + 1))
                else:
                    pool.wait_ge(sig["o_evac"], v2("o_evac", n + 1))
                pool.tensor_tensor(b_tok[:, n % TI], b_tok[:, n % TI], o_tok[:, n % TI, :], ALU.add)\
                    .then_inc(once["b_sum"], 1)
            add_squares(DEPTH, 1)
            add_squares(DEPTH, 2)

        @block.scalar
        def _(act):
            act.dma_start(cst[:, P:C_END], A["shape_constants"][:, P:C_END]).then_inc(i_load["cst"], 16)
            act.wait_ge(i_clear, 4)
            for row, src in gain_rows_2(A):
                n = src.shape[0]
                dst = v_mla[row:row + n, 1, 0:P]
                if src.shape[1] < P:
                    dst = dst.rearrange("r (a c) -> r a c", a=2)
                    src = bass.AP(src.tensor, src.offset, [[64, n], [0, 2], [1, 64]])
                act.dma_start(dst, src).then_inc(i_load["gains_2"], 16)
            act.wait_ge(i_load["mem"], 16)
            for i in range(TI):
                act.activation(kx_t[:, 4 * i:4 * i + 4, :], prologue_mem[:, i, :].rearrange("p (a b) -> p a b", a=4),
                               ACT.Square, accum_out=row_sum[:, i:i + 1]).then_inc(i_stat, 1)
            act.wait_ge(i_load["cst"], 16)
            act.wait_ge(i_stat, TI)
            act.activation(root[:, 0:TI], row_sum[:, 0:TI], ACT.Sqrt, scale=1.0 / D, bias=eps)\
                .then_inc(i_stat, 1)

            def scaled_hi(layer, first, src, dst, gain, n=8, src_ready=None, square=None, gains=g_cur):
                for k in range(n):
                    if src_ready is not None:
                        src_ready(k)
                    name = "act_hi" if n == 8 else "c_hi"
                    act.activation(dst[:, k], src[:, k], ACT.Copy, scale=gains[:, gain + k:gain + k + 1])\
                        .then_inc(sig[name], 1)
                    if square is not None and k % 2:
                        squares(layer, square, k // 2, src[:, k - 1:k + 1])

            def squares(layer, norm, j, src):
                if j >= 2:
                    act.wait_ge(sig["sumsq"], value("sumsq", layer, 2 * norm + j - 1))
                act.activation(halves(sumsq[:, :] if j == 0 else sq_next[:, :]), src, ACT.Square)\
                    .then_inc(sig["square"], 1)

            def root_of(layer, stat, use, width, d=D):
                act.wait_ge(sig["stat_mm"], value("stat_mm", layer, stat + 1))
                act.activation(root[:, 0:width], bank(use, layer)[:, 0:width], ACT.Sqrt, scale=1.0 / d, bias=eps)\
                    .then_inc(sig["root"], 1)

            def branch_out(layer, norm, first_slab, first, per_bank=1):
                name = {2: "mix", 4: "xo", 6: "down"}[norm]
                pos = {2: 1, 4: 3, 6: 5}[norm]
                for b in range(4):
                    s = first_slab + per_bank * b
                    for c in range(per_bank):
                        if (s + c) + 3 <= 66:
                            split_hi(act, layer, s + c + 3)
                    act.wait_ge(sig["slab_used"], value("slab_used", layer, s + per_bank))
                    squares(layer, pos, b, halves(bank(f"{name}{b}")[:, :]))
                    act.activation(qk_dil[:, 2 * b:2 * b + 2, :], halves(bank(f"{name}{b}")[:, :]), ACT.Copy)\
                        .then_inc(sig["a_evac"], 1)

            def exps(layer, u, heads, keys, col, src=None, step=1):
                act.wait_ge(sig["neg_max"], value("neg_max", layer, u + 1))
                if src is not None:
                    act.wait_ge(sig["p_turned"], value("p_turned", layer, u - P_RING + 1))
                w = probs[:, u % P_RING, :].rearrange("p (h k) -> p h k", k=keys)
                for h in range(heads):
                    r = w[:, h, :] if src is None else src[:, h, :]
                    c = slice(col + step * h, col + step * h + 1)
                    ins = act.activation(w[:, h, :], r, ACT.Exp, bias=neg_max[:, c], accum_out=row_sum[:, c])
                ins.then_inc(sig["probs"], 1)

            def causal_exps(layer, u):
                i, heads, kt = (unit_2 if second(layer) else unit)(u % 6)
                exps(layer, u, len(heads), P * kt, 16 * (u // 6) + 8 * i + heads[0], step=heads.step)

            def squared_up(layer, b):
                act.wait_ge(sig["up_scaled"], value("up_scaled", layer, b + 1))
                if b >= PT_RING:
                    act.wait_ge(sig["h_lo"], value("h_lo", layer, b - PT_RING + 1))
                act.activation(p_t[:, b % PT_RING, :], probs[:, b % P_RING, :], ACT.Square)
                act.activation(h_hi[:, 2 * b:2 * b + 2, :], halves(probs[:, b % P_RING, :]), ACT.Square)\
                    .then_inc(sig["h_sq"], 1)

            def turned_out(layer, u):
                act.wait_ge(sig["p_turned"], value("p_turned", layer, u + 1))
                if u >= PT_RING:
                    act.wait_ge(sig["pv"], value("pv", layer, u - PT_RING + 1))
                act.activation(p_t[:, u % PT_RING, :], bank(f"turn{u}", layer)[:, :], ACT.Copy)\
                    .then_inc(sig["pt_a"], 1)

            def o_part(layer, b, tile0, i):
                act.wait_ge(sig["o_turned"], value("o_turned", layer, b + 1))
                act.activation(o_hi[:, tile0:tile0 + 4, P * i:P * i + P],
                               bank(f"ot{b}", layer)[:, :].rearrange("p (a t) -> p a t", a=4), ACT.Copy)\
                    .then_inc(sig["o_hi"], 1)

            act.wait_ge(i_evac, 5)
            scaled_hi(0, 0, x_t, act_hi, 0, square=0, gains=g_pre[:, 0, :])
            split_hi(act, 0, 0)
            split_hi(act, 0, 1)
            for b in range(4):
                act.wait_ge(i_turned, 6 + b)
                act.activation(mem_t[:, 2 * b:2 * b + 2, :], halves(banks[4 + b][:, :]), ACT.Copy)\
                    .then_inc(i_mem_evac, 1)
            split_hi(act, 0, 2)
            act.wait_ge(i_arg, 1)
            act.activation(rope[:, :], rope_k[:, :], ACT.Sin).then_inc(i_sin, 1)
            act.wait_ge(i_evac, 8)
            act.wait_ge(i_mem_evac, 4)
            with act.Fori(0, DEPTH) as layer:
                act.wait_ge(sig["gains"], value("gains", layer, 1))
                split_hi(act, layer, 3)
                root_of(layer, 0, "stat0", T + TI)
                split_hi(act, layer, 4)
                split_hi(act, layer, 5)
                split_hi(act, layer, 6)
                act.wait_ge(sig["z_evac"], value("z_evac", layer, 4))
                act.activation(kx_t[:, 0:5, :], latents[:, 0:5, :], ACT.Square).then_inc(sig["c_square"], 1)
                act.wait_ge(sig["stat_mm"], value("stat_mm", layer, 2))
                act.activation(root[:, 0:T], bank("stat1")[:, 0:T], ACT.Sqrt, scale=1.0 / Q_RANK, bias=eps)
                act.activation(root[:, T:2 * T], bank("stat1")[:, T:2 * T], ACT.Sqrt, scale=1.0 / KV_RANK,
                               bias=eps).then_inc(sig["root"], 1)
                split_hi(act, layer, 7)
                split_hi(act, layer, 8)
                act.wait_ge(sig["c_norm"], value("c_norm", layer, 2))
                scaled_hi(layer, 0, latents, o_hi, G_Q, n=5)
                act.wait_ge(sig["kpe_mm"], value("kpe_mm", layer, 1))
                act.activation(k_t[64:P, :, :], bank("kpe")[64:P, 0:T].unsqueeze(1).broadcast_to([64, HEADS, T]),
                               ACT.Copy).then_inc(sig["kpe"], 1)
                split_hi(act, layer, 9)
                for u in range(4):
                    causal_exps(layer, u)
                    if u in (1, 2):
                        b = u - 1
                        act.wait_ge(sig["slab_used"], value("slab_used", layer, 8 + b))
                        for t in range(TI):
                            act.activation(v_dil[:, t, T * b:T * b + T], bank(f"z{7 + b}")[:, T * t:T * t + T],
                                           ACT.Copy, scale=rstd[:, T + t:T + t + 1]).then_inc(sig["v_evac"], 1)
                        split_hi(act, layer, 10 + b)
                turned_out(layer, 1)
                causal_exps(layer, 4)
                causal_exps(layer, 5)
                act.wait_ge(sig["slab_used"], value("slab_used", layer, 9))
                scaled_hi(layer, 8, mem_t, act_hi, G_MEM)
                split_hi(act, layer, 12)
                split_hi(act, layer, 13)
                turned_out(layer, 3)
                split_hi(act, layer, 14)
                for t in range(TI):
                    if t == 0:
                        act.wait_ge(sig["first_bank"], value("first_bank", layer, 5))
                    act.activation(v_mla[:, t, :], bank(f"uv{t}")[:, :], ACT.Copy).then_inc(sig["v_evac"], 1)
                turned_out(layer, 5)
                for b in range(4):
                    causal_exps(layer, 6 + b)
                    if b == 1:
                        o_part(layer, 0, 4, 0)
                        o_part(layer, 1, 4, 1)
                    if b == 0:
                        split_hi(act, layer, 15)
                    act.wait_ge(sig["slab_used"], value("slab_used", layer, 13 + b))
                    act.activation(kx_t[:, 2 * b:2 * b + 2, :], halves(bank(f"xk{b}")[:, :]), ACT.Copy)\
                        .then_inc(sig["xkv_evac"], 1)
                causal_exps(layer, 10)
                turned_out(layer, 7)
                split_hi(act, layer, 16)
                split_hi(act, layer, 17)
                causal_exps(layer, 11)
                split_hi(act, layer, 18)
                for b in range(4):
                    if b == 3:
                        o_part(layer, 2, 0, 0)
                        o_part(layer, 3, 0, 1)
                    split_hi(act, layer, 19 + b)
                    act.wait_ge(sig["slab_used"], value("slab_used", layer, 17 + b))
                    act.activation(vx[:, :, T * b:T * b + T], halves(bank(f"xv{b}")[:, :]), ACT.Copy)\
                        .then_inc(sig["xkv_evac"], 1)
                    if b < 2:
                        turned_out(layer, 9 + 2 * b)
                branch_out(layer, 2, 20, 0)
                root_of(layer, 2, "stat2", T)
                scaled_hi(layer, 16, x_t, act_hi, G_PRE_X, square=2,
                          src_ready=lambda k: act.wait_ge(sig["x_new"], value("x_new", layer, k + 1)))
                split_hi(act, layer, 27)
                root_of(layer, 3, "stat3", T)
                for s in (28, 29, 30):
                    split_hi(act, layer, s)
                for u in range(12, 16):
                    exps(layer, u, 2, T, 32 + 2 * (u - 12), halves(bank(f"scores{u}")[:, :]))
                for u in (13, 15):
                    turned_out(layer, u)
                for b in range(4, 8):
                    o_part(layer, b, 4 * (b % 2), (b - 4) // 2)
                branch_out(layer, 4, 28, 4)
                root_of(layer, 4, "stat4", T)
                scaled_hi(layer, 24, x_t, act_hi, G_PRE_MLP, square=4,
                          src_ready=lambda k: act.wait_ge(sig["x_new"], value("x_new", layer, 8 + k + 1)))
                root_of(layer, 5, "stat5", T)
                for b in range(16):
                    split_hi(act, layer, 35 + b)
                    squared_up(layer, b)
                branch_out(layer, 6, 48, 8, per_bank=4)
                root_of(layer, 6, "stat6", T)
                act.wait_ge(sig["g_next"], value("g_next", layer, 1))
                scaled_hi(layer, 32, x_t, act_hi, 0, square=6, gains=g_next,
                          src_ready=lambda k: act.wait_ge(sig["x_new"], value("x_new", layer, 16 + k + 1)))
            def head_square(n, src, dst, ready, count):
                act.wait_ge(once[ready], count)
                if n >= 2:
                    act.wait_ge(once["hs_done"], n - 1)
                act.activation(dst(head_sq[:, n % 2, :]), src, ACT.Square).then_inc(once["hs_square"], 1)

            def head_root(n, width, scale, bias):
                act.wait_ge(once["hs_mm"], n + 1)
                act.activation(head_sq[:, n % 2, 0:width], bank(f"hs{n}", DEPTH)[:, 0:width], ACT.Sqrt,
                               scale=scale, bias=bias).then_inc(once["hs_root"], 1)

            def hidden_tanh(kind):
                c = slice(60 * kind, 60 * kind + 60)
                act.wait_ge(once["ch_poly"], kind + 1)
                act.activation(ch_y[:, c], ch_z[:, c], ACT.Tanh, scale=GELU_B).then_inc(once["ch_tanh"], 1)
                act.wait_ge(once["ch_g"], kind + 1)
                act.activation(ch_hi[:, c], ch_z[:, c], ACT.Copy, scale=0.5).then_inc(once["ch_hi"], 1)

            def gelu_in(b):
                dst = (v_dil if b < 2 else vx)[:, :, 256 * (b % 2):256 * (b % 2) + 256]
                act.wait_ge(sig["slab_used"], v2("slab_used", 12 + b))
                for i in range(TI):
                    ins = act.activation(dst[:, i], bank(f"g{b}", DEPTH)[:, T * i:T * i + T], ACT.Copy,
                                         scale=rstd[:, T + i:T + i + 1])
                ins.then_inc(once["g_evac"], 1)
                act.wait_ge(once["g_evac"], b + 1)
                if b >= 2:
                    act.wait_ge(once["g_out"], b - 1)
                act.activation(gelu_part[b % 2], dst, ACT.Square).then_inc(once["g_square"], 1)

            def gelu_tanh(b):
                act.wait_ge(once["g_poly"], b + 1)
                act.activation(gelu_part[b % 2], gelu_part[b % 2], ACT.Tanh, scale=GELU_B)\
                    .then_inc(once["g_tanh"], 1)

            def ab_squares(n):
                if n:
                    act.wait_ge(once["ab_var"], n)
                src = (a_tok if n < 2 else b_tok)[:, n % 2]
                act.activation(flat(rstd_c), src, ACT.Square, accum_out=ab_stat[:, n:n + 1])\
                    .then_inc(once["ab_var"], 1)

            def ab_root(n):
                act.wait_ge(once["ab_var"], 2 * n + 2)
                c = slice(2 * n, 2 * n + 2)
                act.activation(ab_stat[:, c], ab_stat[:, c], ACT.Sqrt, scale=1.0 / 512, bias=eps)\
                    .then_inc(once["ab_root"], 1)

            eps_64, eps_128, eps_4 = (cst[:, C_COL + c:C_COL + c + 1] for c in (5, 6, 7))
            split_hi(act, DEPTH, 3)
            root_of(DEPTH, 0, "stat0", T + TI)
            split_hi(act, DEPTH, 4)
            split_hi(act, DEPTH, 5)
            act.wait_ge(once["mem_loaded"], 16)
            for i in range(TI):
                act.activation(vx[:, i, :], mem_rows_2[:, i], ACT.Square, accum_out=mem_stat[:, i:i + 1])\
                    .then_inc(once["mem_sum"], 1)
            act.wait_ge(once["mem_sum"], TI)
            act.activation(mem_stat[:, 0:2], mem_stat[:, 0:2], ACT.Sqrt, scale=1.0 / D, bias=eps)\
                .then_inc(once["mem_root"], 1)
            act.wait_ge(once["cin"], 1)
            act.activation(cin_hi, cin, ACT.Copy).then_inc(once["cin_hi"], 1)
            head_square(0, k_t[:, 0:2, :], halves, "y_evac", 3)
            split_hi(act, DEPTH, 6)
            head_root(0, 512, 1.0 / 64, eps)
            split_hi(act, DEPTH, 7)
            head_square(1, q_t[:, 0:2, :], halves, "y_evac", 4)
            head_square(2, q_t[:, 2:4, :], halves, "y_evac", 5)
            for n in range(2):
                act.wait_ge(once["sgw_turned"], n + 1)
                act.activation(sg_w[:, 4 * n:4 * n + 4], bank(f"sgw{n}", DEPTH)[:, :].rearrange(
                    "p (g t) -> p g t", g=4), ACT.Copy).then_inc(once["sgw_evac"], 1)
            split_hi(act, DEPTH, 8)
            head_root(1, 512, 1.0, eps_64)
            head_root(2, 512, 1.0, eps_64)
            split_hi(act, DEPTH, 9)
            hidden_tanh(0)
            split_hi(act, DEPTH, 10)
            split_hi(act, DEPTH, 11)
            hidden_tanh(1)
            split_hi(act, DEPTH, 12)
            head_square(3, kc_raw, lambda b: b[:, 0:30], "kc_evac", 1)
            head_root(3, 30, 1.0 / 64, eps)
            causal_exps(DEPTH, 0)
            causal_exps(DEPTH, 1)
            act.wait_ge(sig["slab_used"], v2("slab_used", 11))
            act.wait_ge(once["neg_rstd"], 1)
            for i in range(TI):
                ins = act.activation(gates[:, i], bank("gates", DEPTH)[:, 24 * i:24 * i + 24].rearrange(
                    "p (h b) -> p h b", b=3), ACT.Exp, scale=neg_rstd[:, i:i + 1])
            ins.then_inc(once["gate_exp"], 1)
            split_hi(act, DEPTH, 13)
            causal_exps(DEPTH, 2)
            causal_exps(DEPTH, 3)
            split_hi(act, DEPTH, 14)
            gelu_in(0)
            causal_exps(DEPTH, 4)
            turned_out(DEPTH, 1)
            split_hi(act, DEPTH, 15)
            gelu_in(1)
            causal_exps(DEPTH, 5)
            gelu_tanh(0)
            turned_out(DEPTH, 3)
            gelu_tanh(1)
            split_hi(act, DEPTH, 16)
            turned_out(DEPTH, 5)
            gelu_in(2)
            split_hi(act, DEPTH, 17)
            gelu_in(3)
            act.wait_ge(once["ln_center"], 1)
            for i in range(TI):
                act.activation(head_sq[:, i, :], v_dil[:, i, :], ACT.Square, accum_out=ln_stat[:, 2 + i:3 + i])\
                    .then_inc(once["ln_var"], 1)
            act.wait_ge(once["ln_var"], TI)
            act.activation(ln_stat[:, 2:4], ln_stat[:, 2:4], ACT.Sqrt, scale=1.0 / 512, bias=eps_4)\
                .then_inc(once["ln_root"], 1)
            gelu_tanh(2)
            gelu_tanh(3)
            for v in range(2):
                act.wait_ge(once["c_ready"], v + 1)
                act.activation(c_p[:, v], c_p[:, v], ACT.Exp).then_inc(once["c_exp"], 1)
            act.wait_ge(sig["slab_used"], v2("slab_used", 15))
            for k in range(8):
                act.wait_ge(once["mem_turned"], k // 2 + 1)
                act.activation(act_hi[:, k], bank(f"mem{k // 2}", DEPTH)[:, T * (k % 2):T * (k % 2) + T], ACT.Copy,
                               scale=g_2[:, N_KV + k:N_KV + k + 1]).then_inc(sig["act_hi"], 1)
            causal_exps(DEPTH, 6)
            causal_exps(DEPTH, 7)
            split_hi(act, DEPTH, 18)
            causal_exps(DEPTH, 8)
            causal_exps(DEPTH, 9)
            head_square(4, kx_t[:, 0:2, :], halves, "mk_evac", 1)
            head_square(5, kx_t[:, 2:4, :], halves, "mk_evac", 2)
            split_hi(act, DEPTH, 19)
            head_root(4, 512, 1.0 / P, eps)
            head_root(5, 512, 1.0 / P, eps)
            turned_out(DEPTH, 7)
            causal_exps(DEPTH, 10)
            causal_exps(DEPTH, 11)
            turned_out(DEPTH, 9)
            split_hi(act, DEPTH, 20)
            for n in range(2):
                act.wait_ge(sig["slab_used"], v2("slab_used", 18 + n))
                act.activation(mem_v[:, :, T * n:T * n + T], halves(bank(f"mv{n}", DEPTH)[:, :]), ACT.Copy)\
                    .then_inc(once["mv_evac"], 1)
                if n == 0:
                    turned_out(DEPTH, 11)
                    act.wait_ge(once["sgu_out"], TI)
                    ab_squares(0)
                    ab_squares(1)
                    ab_root(0)
            split_hi(act, DEPTH, 21)
            for n in range(TI):
                act.wait_ge(once["b_sum"], TI + n + 1)
                ab_squares(2 + n)
            ab_root(1)
            for b in range(4):
                o_part(DEPTH, b, 4 * (b // 2), b % 2)

            def updated(after, splits):
                def ready(k):
                    if k % 2 == 0:
                        for s in splits[k // 2]:
                            split_hi(act, DEPTH, s)
                        act.wait_ge(once["w_evac"], after + k // 2 + 1)
                return ready

            scaled_hi(DEPTH, 16, x_t, act_hi, N_MEM, square=1, gains=g_2,
                      src_ready=updated(0, [[22], [23], [24], [25]]))
            root_of(DEPTH, 1, "stat1", T)
            split_hi(act, DEPTH, 26)
            head_square(6, q_t[:, 0:2, :], halves, "mq_evac", 1)
            head_square(7, q_t[:, 2:4, :], halves, "mq_evac", 2)
            head_root(6, 512, 1.0, eps_128)
            head_root(7, 512, 1.0, eps_128)
            split_hi(act, DEPTH, 27)
            for u in range(12, 16):
                exps(DEPTH, u, 2, T, 32 + 2 * (u - 12), halves(bank(f"scores{u}", DEPTH)[:, :]))
            for u in (13, 15):
                turned_out(DEPTH, u)
            for b in range(4, 6):
                o_part(DEPTH, b, 0, b - 4)
            scaled_hi(DEPTH, 24, x_t, act_hi, N_FFN, square=2, gains=g_2,
                      src_ready=updated(4, [[], [28], [], [29]]))
            root_of(DEPTH, 2, "stat2", T)
            for b in range(16):
                split_hi(act, DEPTH, 30 + b)
                squared_up(DEPTH, b)

            def rows_out(b):
                act.wait_ge(once["out_turned"], b + 1)
                act.activation(out_rows[:, b], halves(bank(f"out{b}", DEPTH)[:, :]), ACT.Copy)\
                    .then_inc(once["out_evac"], 1)

            for s in range(46, 59):
                split_hi(act, DEPTH, s)
                if s in (53, 57):
                    rows_out((s - 53) // 4)
            rows_out(2)
            rows_out(3)

        @block.vector
        def _(dve):
            step = [0]

            def chained(ins):
                step[0] += 1
                ins.then_inc(i_step, 1)
                dve.wait_ge(i_step, step[0])

            dve.wait_ge(i_load["cst"], 16)
            dve.wait_ge(i_load["pos"], 16)
            col = cst[:, C_COL:C_COL + 8]
            ang, turns, r = rope, rope_q, rope_k
            chained(dve.tensor_copy(ang[:, :], vx[:, 0, 0:T].bitcast(I32)))
            chained(dve.tensor_scalar(ang[:, :], ang[:, :], col[:, 0:1], None, ALU.mult))
            chained(dve.tensor_scalar(turns[:, :], ang[:, :], 1.0 / (2 * np.pi), None, ALU.mult))
            magic = 12582912.0
            chained(dve.tensor_scalar(turns[:, :], turns[:, :], magic, None, ALU.add))
            chained(dve.tensor_scalar(turns[:, :], turns[:, :], magic, None, ALU.subtract))
            c1, c2 = 6.28125, 2029.0 / 2 ** 20
            c3 = 2 * np.pi - c1 - c2
            for n, c in enumerate((c1, c2, c3)):
                chained(dve.scalar_tensor_tensor(r[:, :], turns[:, :], -c, ang[:, :] if n == 0 else r[:, :],
                                                 ALU.mult, ALU.add))
            chained(dve.tensor_scalar(r[:, :], r[:, :], 3.1415925, -3.1415925, ALU.min, ALU.max))
            chained(dve.tensor_scalar(ang[:, :], r[:, :], -1.0, None, ALU.mult))
            chained(dve.tensor_tensor(ang[:, :], r[:, :], ang[:, :], ALU.max))
            chained(dve.tensor_scalar(ang[:, :], ang[:, :], col[:, 1:2], col[:, 3:4], ALU.mult, ALU.add))
            dve.scalar_tensor_tensor(r[:, :], r[:, :], col[:, 2:3], ang[:, :], ALU.mult, ALU.add)\
                .then_inc(i_arg, 1)
            for b in range(4):
                dve.wait_ge(i_turned, b + 1)
                dve.tensor_copy(x_t[:, 2 * b:2 * b + 2, :], halves(banks[b][:, :])).then_inc(i_evac, 1)
            dve.wait_ge(i_turned, 5)
            dve.tensor_copy(g_pre[:, 0:DEPTH, :], banks[6][:, 0:2 * P].rearrange("p (l g) -> p l g", l=DEPTH)[:, :, 0:8])\
                .then_inc(i_evac, 1)
            dve.wait_ge(i_stat, TI + 1)
            dve.reciprocal(row_inv[:, 0:TI], root[:, 0:TI]).then_inc(i_inv, 1)
            dve.wait_ge(i_inv, 1)
            for i in range(TI):
                dve.tensor_scalar(prologue_mem[:, i, :], prologue_mem[:, i, :], row_inv[:, i:i + 1], None, ALU.mult)\
                    .then_inc(i_scaled, 1)

            def inverse_root(layer, stat, dst, src):
                dve.wait_ge(sig["root"], value("root", layer, stat + 1))
                dve.reciprocal(dst, src).then_inc(sig["rstd"], 1)
                dve.wait_ge(sig["rstd"], value("rstd", layer, stat + 1))

            def rest(layer, name, n, src, gain, hi, lo, gains=g_cur):
                hi_name = "act_hi" if name == "act_lo" else "c_hi"
                k = (n - 1) % 8
                dve.wait_ge(sig[hi_name], value(hi_name, layer, n))
                dve.scalar_tensor_tensor(lo[:, k], src[:, k], gains[:, gain + k:gain + k + 1],
                                         hi[:, k].bitcast(F32), ALU.mult, ALU.subtract).then_inc(sig[name], 1)

            def scaled(layer, use, dst, scale, slab=None, cols=None):
                if slab is not None:
                    dve.wait_ge(sig["slab_used"], value("slab_used", layer, slab + 1))
                b = bank(use)[:, :]
                dve.scalar_tensor_tensor(dst, halves(b), scale, twice(rstd[:, 0:T]), ALU.mult, ALU.mult)\
                    .then_inc(sig["z_evac"], 1)

            def bias_and_max(layer, u):
                i, heads, kt = (unit_2 if second(layer) else unit)(u % 6)
                n, w, step = len(heads), P * kt, heads.step
                dve.wait_ge(sig["scores"], value("scores", layer, u + 1))
                if u >= P_RING:
                    dve.wait_ge(sig["p_turned"], value("p_turned", layer, u - P_RING + 1))
                dst = probs[:, u % P_RING, :].rearrange("p (h k) -> p h k", k=w)
                if u < 6 and not second(layer):
                    table = toep[:, heads[0]:heads[0] + step * (n - 1) + 1:step, T - w:T]
                else:
                    table = causal[:, T - w:T].unsqueeze(1).broadcast_to([P, n, w])
                dve.tensor_tensor(dst, bank(f"scores{u}", layer)[:, :].rearrange("p (h k) -> p h k", k=w), table,
                                  ALU.add).then_inc(sig["biased"], 1)
                dve.wait_ge(sig["biased"], value("biased", layer, u + 1))
                c = 16 * (u // 6) + 8 * i + heads[0]
                dve.tensor_reduce(neg_max[:, c:c + step * (n - 1) + 1:step], dst, AX.X, ALU.max, negate=True)\
                    .then_inc(sig["neg_max"], 1)

            def turned_out(layer, u):
                dve.wait_ge(sig["p_turned"], value("p_turned", layer, u + 1))
                if u >= PT_RING:
                    dve.wait_ge(sig["pv"], value("pv", layer, u - PT_RING + 1))
                dve.tensor_copy(p_t[:, u % PT_RING, :], bank(f"turn{u}", layer)[:, :]).then_inc(sig["pt_v"], 1)

            def o_out(layer, b, u, col, n):
                dve.wait_ge(sig["probs"], value("probs", layer, u + 1))
                dve.reciprocal(row_inv[:, col:col + n], row_sum[:, col:col + n]).then_inc(sig["rinv"], 1)
                dve.wait_ge(sig["rinv"], value("rinv", layer, b + 1))
                dve.wait_ge(sig["pv"], value("pv", layer, u + 1))
                if b >= TI:
                    dve.wait_ge(sig["o_turned"], value("o_turned", layer, b - TI + 1))
                w = 512 // n
                dve.tensor_tensor(o_tok[:, b % TI, :].rearrange("p (h d) -> p h d", h=n),
                                  bank(f"o{b}", layer)[:, :].rearrange("p (h d) -> p h d", h=n),
                                  row_inv[:, col:col + n].unsqueeze(2).broadcast_to([P, n, w]), ALU.mult)\
                    .then_inc(sig["o_evac"], 1)

            def o_rest(layer, b, tile0, i):
                dve.wait_ge(sig["o_hi"], value("o_hi", layer, b + 1))
                t = slice(P * i, P * i + P)
                dve.tensor_tensor(o_lo[:, tile0:tile0 + 4, t], bank(f"ot{b}", layer)[:, :].rearrange(
                    "p (a t) -> p a t", a=4), o_hi[:, tile0:tile0 + 4, t].bitcast(F32), ALU.subtract)\
                    .then_inc(sig["o_lo"], 1)

            def residual(layer, stat, norm, a_first, gain, next_first, next_gain, next_gains=g_cur):
                inverse_root(layer, stat, rstd[:, 0:T], root[:, 0:T])
                def over_norm(j):
                    dve.wait_ge(sig["a_evac"], value("a_evac", layer, a_first + j + 1))
                    pair = qk_dil[:, 2 * j:2 * j + 2, :]
                    dve.tensor_tensor(pair, pair, twice(rstd[:, 0:T]), ALU.mult).then_inc(sig["x_part"], 1)

                over_norm(0)
                for j in range(4):
                    dve.wait_ge(sig["x_part"], value("x_part", layer, 4 * norm + j + 1))
                    for k in (2 * j, 2 * j + 1):
                        dve.scalar_tensor_tensor(x_t[:, k], qk_dil[:, k], g_cur[:, gain + k:gain + k + 1],
                                                 x_t[:, k], ALU.mult, ALU.add).then_inc(sig["x_new"], 1)
                    if j < 3:
                        over_norm(j + 1)
                    for k in (2 * j, 2 * j + 1):
                        rest(layer, "act_lo", next_first + k + 1, x_t, next_gain, act_hi, act_lo, next_gains)

            def hidden_up(layer, used, split):
                for b in range(17):
                    if b < 16:
                        dve.wait_ge(sig["slab_used"], value("slab_used", layer, used + b))
                        if b >= P_RING:
                            dve.wait_ge(sig["h_sq"], value("h_sq", layer, b - P_RING + 1))
                        dve.scalar_tensor_tensor(halves(probs[:, b % P_RING, :]), halves(bank(f"up{b}", layer)[:, :]),
                                                 0.0, twice(rstd[:, 0:T]), ALU.max, ALU.mult)\
                            .then_inc(sig["up_scaled"], 1)
                        split_lo(dve, layer, split + b)
                    if b:
                        dve.wait_ge(sig["h_sq"], value("h_sq", layer, b))
                        dve.tensor_tensor(h_lo[:, 2 * b - 2:2 * b, :], halves(p_t[:, (b - 1) % PT_RING, :]),
                                          h_hi[:, 2 * b - 2:2 * b, :].bitcast(F32), ALU.subtract)\
                            .then_inc(sig["h_lo"], 1)

            for k in range(8):
                rest(0, "act_lo", k + 1, x_t, 0, act_hi, act_lo, g_pre[:, 0, :])
            split_lo(dve, 0, 0)
            dve.wait_ge(i_turned, 10)
            rows = banks[0][:, 0:2 * P].rearrange("p (l g) -> p l g", l=DEPTH)
            dve.tensor_copy(g_all[:, :, :], rows[:, :, 0:G_PITCH]).then_inc(i_evac, 1)
            dve.wait_ge(i_turned, 11)
            dve.tensor_copy(qk_dil[0:HEADS, 0:2, :], halves(banks[1][0:HEADS, :])).then_inc(i_evac, 1)
            dve.wait_ge(i_turned, 12)
            dve.tensor_copy(g_pre[:, DEPTH, :], banks[2][:, N_MIX:N_MIX + 8])
            dve.tensor_copy(g_2[:, :], banks[2][:, 0:N_ROWS]).then_inc(i_evac, 1)
            split_lo(dve, 0, 1)
            split_lo(dve, 0, 2)
            dve.wait_ge(i_sin, 1)
            chained(dve.memset(rope[0:64, :], 1.0))
            chained(dve.tensor_scalar(rope_q[:, :], rope[:, :], MLA_SCALE, None, ALU.mult))
            dve.wait_ge(i_evac, 8)
            with dve.Fori(0, DEPTH) as layer:
                dve.tensor_copy(g_cur[:, :], g_all[:, layer, :]).then_inc(sig["gains"], 1)
                dve.wait_ge(sig["gains"], value("gains", layer, 1))
                split_lo(dve, layer, 3)
                inverse_root(layer, 0, rstd[:, :], root[:, 0:T + TI])
                dve.tensor_tensor(rope_k[:, :], rope[:, :], rstd[:, 0:T], ALU.mult).then_inc(sig["rope_k"], 1)
                scaled(layer, "z0", latents[:, 0:2, :], 1.0, 0)
                scaled(layer, "z1", latents[:, 2:4, :], 1.0, 1)
                split_lo(dve, layer, 4)
                dve.wait_ge(i_load["rows"], 16)
                scaled(layer, "z2", qk_dil[:, 0:2, :], DIL_SCALE, 2)
                split_lo(dve, layer, 5)
                dve.wait_ge(sig["slab_used"], value("slab_used", layer, 4))
                dve.tensor_tensor(latents[:, 4, :], bank("z3")[:, 0:T], rstd[:, 0:T], ALU.mult)\
                    .then_inc(sig["z_evac"], 1)
                dve.wait_ge(sig["rope_k"], value("rope_k", layer, 1))
                dve.tensor_tensor(latents[:, 5, :], bank("z3")[:, T:2 * T], rope_k[:, :], ALU.mult)\
                    .then_inc(sig["z_evac"], 1)
                split_lo(dve, layer, 6)
                scaled(layer, "z4", qk_dil[:, 2:4, :], DIL_SCALE, 4)
                split_lo(dve, layer, 7)
                scaled(layer, "z5", qk_dil[:, 4:6, :], 1.0, 5)
                split_lo(dve, layer, 8)
                scaled(layer, "z6", qk_dil[:, 6:8, :], 1.0, 6)
                inverse_root(layer, 1, rstd_c[:, :, :], halves(root[:, :]))
                for n, (a, b) in enumerate(((0, 3), (3, 5))):
                    dve.tensor_tensor(latents[:, a:b, :], latents[:, a:b, :],
                                      rstd_c[:, n, :].unsqueeze(1).broadcast_to([P, b - a, T]), ALU.mult)\
                        .then_inc(sig["c_norm"], 1)
                dve.wait_ge(sig["c_norm"], value("c_norm", layer, 2))
                for k in range(5):
                    rest(layer, "c_lo", k + 1, latents, G_Q, o_hi, o_lo)
                split_lo(dve, layer, 9)
                dve.wait_ge(i_load["toep"], 16)
                def query_bank(b):
                    if b % 2 == 0:
                        dve.wait_ge(sig["first_bank"], value("first_bank", layer, b // 2 + 1))
                    else:
                        dve.wait_ge(sig["slab_used"], value("slab_used", layer, 10 + b // 2))
                    dve.tensor_tensor(q_t[:, 2 * b:2 * b + 2, :], halves(bank(f"uq{b}")[:, :]), twice(rope_q[:, :]),
                                      ALU.mult).then_inc(sig["z_evac"], 1)

                for u in range(4):
                    bias_and_max(layer, u)
                split_lo(dve, layer, 10)
                turned_out(layer, 0)
                bias_and_max(layer, 4)
                split_lo(dve, layer, 11)
                query_bank(0)
                query_bank(1)
                bias_and_max(layer, 5)
                turned_out(layer, 2)
                for k in range(8):
                    rest(layer, "act_lo", 8 + k + 1, mem_t, G_MEM, act_hi, act_lo)
                split_lo(dve, layer, 12)

                o_out(layer, 0, 1, 0, 8)
                query_bank(2)
                query_bank(3)
                split_lo(dve, layer, 13)
                turned_out(layer, 4)
                for b in range(2):
                    dve.wait_ge(sig["first_bank"], value("first_bank", layer, 3 + b))
                    for half in range(2):
                        src = halves(bank(f"uk{b}")[64 * half:64 * half + 64, :])
                        dst = k_t[0:64, 4 * b:4 * b + 4, :].rearrange("p (m a) t -> p m a t", a=2)[:, :, half, :]
                        dve.tensor_copy(dst, src).then_inc(sig["z_evac"], 1)
                split_lo(dve, layer, 14)
                o_out(layer, 1, 5, 8, 8)
                bias_and_max(layer, 6)
                bias_and_max(layer, 7)
                split_lo(dve, layer, 15)
                bias_and_max(layer, 8)
                o_rest(layer, 0, 4, 0)
                o_rest(layer, 1, 4, 1)
                bias_and_max(layer, 9)
                turned_out(layer, 6)
                bias_and_max(layer, 10)
                bias_and_max(layer, 11)
                turned_out(layer, 8)
                split_lo(dve, layer, 16)
                split_lo(dve, layer, 17)
                o_out(layer, 2, 7, 16, 8)
                split_lo(dve, layer, 18)
                turned_out(layer, 10)
                split_lo(dve, layer, 19)
                split_lo(dve, layer, 20)
                o_out(layer, 3, 11, 24, 8)
                split_lo(dve, layer, 21)
                o_rest(layer, 2, 0, 0)
                o_rest(layer, 3, 0, 1)
                split_lo(dve, layer, 22)
                for s in range(23, 27):
                    split_lo(dve, layer, s)
                residual(layer, 2, 0, 0, G_POST_MIX, 16, G_PRE_X)
                split_lo(dve, layer, 27)
                inverse_root(layer, 3, rstd[:, 0:T], root[:, 0:T])
                for b in range(4):
                    scaled(layer, f"xq{b}", q_t[:, 2 * b:2 * b + 2, :], X_SCALE, 24 + b)
                    if b == 2:
                        split_lo(dve, layer, 28)
                for u in range(12, 16):
                    dve.wait_ge(sig["scores"], value("scores", layer, u + 1))
                    c = 32 + 2 * (u - 12)
                    dve.tensor_reduce(neg_max[:, c:c + 2], halves(bank(f"scores{u}")[:, :]), AX.X, ALU.max,
                                      negate=True).then_inc(sig["neg_max"], 1)
                    if u in (12, 13):
                        split_lo(dve, layer, 17 + u)
                turned_out(layer, 12)
                turned_out(layer, 14)
                for u in range(12, 16):
                    o_out(layer, u - 8, u, 32 + 2 * (u - 12), 2)
                    if u > 12:
                        o_rest(layer, u - 9, 4 * ((u - 13) % 2), (u - 13) // 2)
                o_rest(layer, 7, 4, 1)
                for s in range(31, 35):
                    split_lo(dve, layer, s)
                residual(layer, 4, 1, 4, G_POST_X, 24, G_PRE_MLP)
                inverse_root(layer, 5, rstd[:, 0:T], root[:, 0:T])
                hidden_up(layer, 33, 35)
                for s in range(51, 67):
                    split_lo(dve, layer, s)
                dve.tensor_copy(g_next[:, :], g_pre[:, layer + 1, :]).then_inc(sig["g_next"], 1)
                dve.wait_ge(sig["g_next"], value("g_next", layer, 1))
                residual(layer, 6, 2, 8, G_POST_MLP, 32, 0, g_next)
            chain = [0]

            def then_next(ins):
                chain[0] += 1
                ins.then_inc(once["step"], 1)
                dve.wait_ge(once["step"], chain[0])

            def head_norms(n, targets, width):
                r = head_sq[:, n % 2, 0:width]
                dve.wait_ge(once["hs_root"], n + 1)
                dve.reciprocal(r, r).then_inc(once["hs_rstd"], 1)
                dve.wait_ge(once["hs_rstd"], n + 1)
                for dst, src, gain, a, b in targets:
                    rr = r[:, a:b]
                    if len(dst.shape) == 3:
                        rr = rr.rearrange("p (a t) -> p a t", a=dst.shape[1])
                    ins = dve.scalar_tensor_tensor(dst, src, g_2[:, gain:gain + 1], rr, ALU.mult, ALU.mult)
                ins.then_inc(once["hs_done"], 1)

            def key_value(n):
                dve.wait_ge(sig["slab_used"], v2("slab_used", n + 2))
                b = bank(f"y{n + 1}", DEPTH)
                dve.tensor_tensor(k_t[:, n, :], b[:, 0:T], rstd[:, 0:T], ALU.mult)
                dve.tensor_tensor(v_mla[:, :, P * n:P * n + P], b[:, T:2 * T].rearrange("p (i c) -> p i c", i=TI),
                                  rstd[:, T:T + TI].unsqueeze(2).broadcast_to([P, TI, P]), ALU.mult)\
                    .then_inc(once["y_evac"], 1)

            def queries(n):
                dve.wait_ge(sig["slab_used"], v2("slab_used", n + 4))
                dve.tensor_tensor(q_t[:, 2 * n:2 * n + 2, :], halves(bank(f"y{n + 3}", DEPTH)[:, :]),
                                  twice(rstd[:, 0:T]), ALU.mult).then_inc(once["y_evac"], 1)

            def hidden(kind):
                c = slice(60 * kind, 60 * kind + 60)
                x, y, z = ch_x[:, c], ch_y[:, c], ch_z[:, c]
                dve.wait_ge(sig["slab_used"], v2("slab_used", 7 + 2 * kind))
                dve.tensor_tensor(x.rearrange("p (a n) -> p a n", a=2),
                                  bank(f"ch{kind}", DEPTH)[:, 0:60].rearrange("p (a n) -> p a n", a=2),
                                  g_2[:, N_B1 + 2 * kind:N_B1 + 2 * kind + 2].unsqueeze(2).broadcast_to([P, 2, 30]),
                                  ALU.add).then_inc(once["ch_evac"], 1)
                dve.wait_ge(once["ch_evac"], kind + 1)
                then_next(dve.tensor_tensor(y, x, x, ALU.mult))
                then_next(dve.tensor_scalar(y, y, GELU_A, 1.0, ALU.mult, ALU.add))
                dve.tensor_tensor(z, y, x, ALU.mult).then_inc(once["ch_poly"], 1)
                dve.wait_ge(once["ch_tanh"], kind + 1)
                dve.scalar_tensor_tensor(z, y, 1.0, x, ALU.add, ALU.mult).then_inc(once["ch_g"], 1)
                dve.wait_ge(once["ch_hi"], kind + 1)
                dve.scalar_tensor_tensor(ch_lo[:, c], z, 0.5, ch_hi[:, c].bitcast(F32), ALU.mult, ALU.subtract)\
                    .then_inc(once["ch_lo"], 1)

            def gelu_poly(b):
                part = gelu_part[b % 2]
                x = (v_dil if b < 2 else vx)[:, :, 256 * (b % 2):256 * (b % 2) + 256]
                dve.wait_ge(once["g_square"], b + 1)
                then_next(dve.tensor_scalar(part, part, GELU_A, 1.0, ALU.mult, ALU.add))
                dve.tensor_tensor(part, part, x, ALU.mult).then_inc(once["g_poly"], 1)

            def gelu_out(b):
                x = (v_dil if b < 2 else vx)[:, :, 256 * (b % 2):256 * (b % 2) + 256]
                dve.wait_ge(once["g_tanh"], b + 1)
                dve.scalar_tensor_tensor(x, gelu_part[b % 2], 1.0, x, ALU.add, ALU.mult).then_inc(once["g_out"], 1)

            def per_head(ap):
                return ap.rearrange("p (h d) -> p h d", h=HEADS)

            def branch(i, o, weights, first):
                dst = b_tok[:, i] if first else o_tok[:, i, :]
                return dve.tensor_tensor(per_head(dst), per_head(o), weights.unsqueeze(2).broadcast_to([P, HEADS, 64]),
                                         ALU.mult)

            def attention_out(b):
                n, i = b // 2 + 1, b % 2
                c = slice(8 * b, 8 * b + 8)
                u = 6 * (b // 2) + (1 if i == 0 else 5)
                dve.wait_ge(sig["probs"], v2("probs", u + 1))
                dve.reciprocal(row_inv[:, c], row_sum[:, c]).then_inc(sig["rinv"], 1)
                dve.wait_ge(sig["rinv"], v2("rinv", b + 1))
                then_next(dve.tensor_tensor(coef[:, n, i], gates[:, i, :, n], row_inv[:, c], ALU.mult))
                dve.wait_ge(sig["pv"], v2("pv", u + 1))
                if b >= 2:
                    dve.wait_ge(once["b_sum"], i + 1)
                branch(i, bank(f"o{b}", DEPTH)[:, :], coef[:, n, i], b < 2).then_inc(sig["o_evac"], 1)

            def update(b, after, n, done, count):
                dve.wait_ge(sig[done], v2(done, count))
                pair = x_t[:, 2 * b:2 * b + 2, :]
                dve.tensor_tensor(pair, halves(bank(after + str(b), DEPTH)[:, :]), pair, ALU.add)\
                    .then_inc(once["w_evac"], 1)
                dve.wait_ge(once["w_evac"], n + b + 1)

            def rests(b, first, gain):
                for k in (2 * b, 2 * b + 1):
                    rest(DEPTH, "act_lo", first + k + 1, x_t, gain, act_hi, act_lo, gains=g_2)

            split_lo(dve, DEPTH, 3)
            inverse_root(DEPTH, 0, rstd[:, :], root[:, 0:T + TI])
            dve.tensor_scalar(neg_rstd, rstd[:, T:T + TI], -1.0, None, ALU.mult).then_inc(once["neg_rstd"], 1)
            dve.wait_ge(sig["slab_used"], v2("slab_used", 1))
            for v in range(2):
                for odd in range(2):
                    r = slice(64 * v, 64 * v + 64)
                    ins = dve.tensor_tensor(k_t[64 * odd:64 * odd + 64, 2 + v:5 + v:2, 0:T - odd],
                                            halves(bank("y0", DEPTH)[r, :])[:, :, odd:T],
                                            rstd[r, odd:T].unsqueeze(1).broadcast_to([64, 2, T - odd]), ALU.mult)
            ins.then_inc(once["y_evac"], 1)
            dve.wait_ge(once["y_evac"], 1)
            for kind in range(2):
                for v in range(2):
                    src = k_t[:, 2 + 2 * kind + v, :]
                    src = bass.AP(src.tensor, src.offset, [src.ap[0], [2, 16], [16, N_CMP]])
                    dst = cin.rearrange("p (a m v n) -> p a m v n", a=2, m=16, v=2)[:, kind, :, v]
                    pos = g_2[:, N_POS + 16 * kind:N_POS + 16 * kind + 16]
                    ins = dve.tensor_tensor(dst, src, pos.unsqueeze(2).broadcast_to([P, 16, N_CMP]), ALU.add)
            ins.then_inc(once["cin"], 1)
            split_lo(dve, DEPTH, 4)
            key_value(0)
            key_value(1)
            split_lo(dve, DEPTH, 5)
            dve.wait_ge(once["mem_root"], 1)
            dve.reciprocal(mem_stat[:, 2:4], mem_stat[:, 0:2]).then_inc(once["mem_inv"], 1)
            dve.wait_ge(once["cin_hi"], 1)
            dve.tensor_tensor(cin_lo, cin, cin_hi.bitcast(F32), ALU.subtract).then_inc(once["cin_lo"], 1)
            dve.wait_ge(once["sgw_loaded"], 16)
            dve.scalar_tensor_tensor(sg_w, causal[:, P:T].unsqueeze(1).broadcast_to([P, 8, P]), -1.0, sg_w,
                                     ALU.is_ge, ALU.mult).then_inc(once["sgw_masked"], 1)
            then_next(dve.memset(flat(qk_dil)[:, 1024:1856], 0.0))
            split_lo(dve, DEPTH, 6)
            queries(0)
            head_norms(0, [(k_t[:, n, :], k_t[:, n, :], N_K + 1 + n, T * n, T * n + T) for n in range(2)], 512)
            split_lo(dve, DEPTH, 7)
            queries(1)
            split_lo(dve, DEPTH, 8)
            for n in range(2):
                head_norms(1 + n, [(q_t[:, 2 * n:2 * n + 2, :], q_t[:, 2 * n:2 * n + 2, :], N_Q, 0, 512)], 512)
            split_lo(dve, DEPTH, 9)
            hidden(0)
            split_lo(dve, DEPTH, 10)
            split_lo(dve, DEPTH, 11)
            hidden(1)
            split_lo(dve, DEPTH, 12)
            dve.wait_ge(sig["slab_used"], v2("slab_used", 10))
            kcb = bank("kc", DEPTH)
            dve.tensor_scalar(kc_raw, kcb[:, 0:30], g_2[:, N_B2:N_B2 + 1], None, ALU.add)\
                .then_inc(once["kc_evac"], 1)
            for v in range(2):
                dve.tensor_scalar(c_z[:, v].rearrange("p (a n) -> p a n", a=4)[:, :, 0:N_CMP],
                                  kcb[:, 64 + N_CMP * v:64 + N_CMP * v + N_CMP].unsqueeze(1).broadcast_to([P, 4, N_CMP]),
                                  g_2[:, N_B2 + 1:N_B2 + 2], None, ALU.add).then_inc(once["kc_evac"], 1)
            head_norms(3, [(kc[:, :, 0:N_CMP], kc_raw.rearrange("p (v n) -> p v n", v=2), N_K, 0, 30)], 30)
            for u in range(4):
                bias_and_max(DEPTH, u)
            split_lo(dve, DEPTH, 13)
            flat_gates = rope[:, 128:176]
            dve.wait_ge(once["gate_exp"], 1)
            then_next(dve.tensor_scalar(flat_gates, flat_gates, 1.0, None, ALU.add))
            then_next(dve.reciprocal(flat_gates, flat_gates))
            turned_out(DEPTH, 0)
            split_lo(dve, DEPTH, 14)
            bias_and_max(DEPTH, 4)
            gelu_poly(0)
            bias_and_max(DEPTH, 5)
            turned_out(DEPTH, 2)
            split_lo(dve, DEPTH, 15)
            gelu_poly(1)
            attention_out(0)
            turned_out(DEPTH, 4)
            gelu_out(0)
            gelu_out(1)
            split_lo(dve, DEPTH, 16)
            dve.wait_ge(once["g_out"], 2)
            then_next(dve.tensor_reduce(ln_stat[:, 0:2], v_dil[:, :, :], AX.X, ALU.add))
            then_next(dve.tensor_scalar(ln_stat[:, 0:2], ln_stat[:, 0:2], -1.0 / 512, None, ALU.mult))
            dve.tensor_tensor(v_dil[:, :, :], v_dil[:, :, :], ln_stat[:, 0:2].unsqueeze(2).broadcast_to([P, TI, 512]),
                              ALU.add).then_inc(once["ln_center"], 1)
            attention_out(1)
            gelu_poly(2)
            split_lo(dve, DEPTH, 17)
            gelu_poly(3)
            dve.wait_ge(once["ln_root"], 1)
            then_next(dve.reciprocal(ln_stat[:, 4:6], ln_stat[:, 2:4]))
            dve.wait_ge(once["ln_loaded"], 32)
            for i in range(TI):
                then_next(dve.scalar_tensor_tensor(v_dil[:, i, :], v_dil[:, i, :], ln_stat[:, 4 + i:5 + i],
                                                   ln_rows[:, 0], ALU.mult, ALU.mult))
            dve.tensor_tensor(v_dil[:, :, :], v_dil[:, :, :], ln_rows[:, 1].unsqueeze(1).broadcast_to([P, TI, 512]),
                              ALU.add).then_inc(once["ln_done"], 1)
            gelu_out(2)
            gelu_out(3)
            dve.wait_ge(once["vturned"], 1)
            for v in range(2):
                ins = dve.tensor_tensor(c_v[:, v].rearrange("p (a d) -> p a d", a=4),
                                        bank("vturn0", DEPTH)[:, P * v:P * v + 64].unsqueeze(1).broadcast_to([P, 4, 64]),
                                        cst[:, C_PART:C_PART + 4].unsqueeze(2).broadcast_to([P, 4, 64]), ALU.mult)
            ins.then_inc(once["vblk"], 1)
            for v in range(2):
                p3 = c_p[:, v].rearrange("p (a n) -> p a n", n=32)
                m = c_max[:, 8 * v:8 * v + 8]
                dve.wait_ge(once["c_scores"], v + 1)
                dve.tensor_tensor(c_p[:, v].rearrange("p (i j n) -> p i j n", i=TI, j=4),
                                  bank(f"cscores{v}", DEPTH)[:, 0:256].rearrange("p (i j n) -> p i j n", i=TI, j=4),
                                  cst[:, C_CMP:C_CMP + 64].rearrange("p (i n) -> p i n", i=TI).unsqueeze(2)
                                  .broadcast_to([P, TI, 4, 32]), ALU.add).then_inc(once["c_biased"], 1)
                dve.wait_ge(once["c_biased"], v + 1)
                then_next(dve.tensor_reduce(m, p3, AX.X, ALU.max, negate=True))
                then_next(dve.tensor_scalar(m, m, 1.0e25, None, ALU.min))
                dve.tensor_tensor(p3, p3, m.unsqueeze(2).broadcast_to([P, 8, 32]), ALU.add)\
                    .then_inc(once["c_ready"], 1)
            for k in range(8):
                dve.wait_ge(sig["act_hi"], v2("act_hi", 10 + k - k % 2))
                dve.scalar_tensor_tensor(act_lo[:, k], bank(f"mem{k // 2}", DEPTH)[:, T * (k % 2):T * (k % 2) + T],
                                         g_2[:, N_KV + k:N_KV + k + 1], act_hi[:, k].bitcast(F32),
                                         ALU.mult, ALU.subtract).then_inc(sig["act_lo"], 1)
            bias_and_max(DEPTH, 6)
            bias_and_max(DEPTH, 7)
            bias_and_max(DEPTH, 8)
            bias_and_max(DEPTH, 9)
            dve.wait_ge(once["c_exp"], 2)
            then_next(dve.tensor_reduce(c_sum, flat(qk_dil)[:, 0:512].rearrange("p (a n) -> p a n", n=32),
                                        AX.X, ALU.add))
            then_next(dve.tensor_scalar(c_sum, c_sum, 0.5, None, ALU.max))
            then_next(dve.reciprocal(c_sum, c_sum))
            for i in range(TI):
                ins = dve.tensor_tensor(coef[:, 0, i].rearrange("p (v j) -> p v j", v=2),
                                        gates[:, i, :, 0].rearrange("p (v j) -> p v j", v=2),
                                        c_sum.rearrange("p (v i j) -> p v i j", v=2, i=TI)[:, :, i], ALU.mult)
            then_next(ins)
            split_lo(dve, DEPTH, 18)

            def memory_keys(n):
                dve.wait_ge(sig["slab_used"], v2("slab_used", 16 + n))
                dve.tensor_copy(kx_t[:, 2 * n:2 * n + 2, :], halves(bank(f"mk{n}", DEPTH)[:, :]))\
                    .then_inc(once["mk_evac"], 1)

            memory_keys(0)
            for i in range(TI):
                dve.wait_ge(once["sgu_mm"], i + 1)
                dve.tensor_tensor(per_head(a_tok[:, i]), per_head(bank(f"sgu{i}", DEPTH)[:, :]),
                                  g_2[:, N_SGB:N_SGB + 8].unsqueeze(2).broadcast_to([P, 8, 64]), ALU.add)\
                    .then_inc(once["sgu_evac"], 1)
                dve.wait_ge(once["sgu_evac"], i + 1)
                dve.scalar_tensor_tensor(a_tok[:, i], vx[:, i, 0:512], 0.5, a_tok[:, i], ALU.mult, ALU.mult)\
                    .then_inc(once["sgu_out"], 1)
            memory_keys(1)
            dve.wait_ge(once["c_turned"], 1)
            dve.tensor_copy(c_pt.rearrange("p v i t -> p (v i t)"), bank("cturn0", DEPTH)[:, :])\
                .then_inc(once["cturn_evac"], 1)
            for i in range(TI):
                dve.wait_ge(once["c_pv"], i + 1)
                branch(i, bank(f"oc{i}", DEPTH)[:, :], coef[:, 0, i], False).then_inc(once["b_part"], 1)
            turned_out(DEPTH, 6)
            bias_and_max(DEPTH, 10)
            bias_and_max(DEPTH, 11)
            turned_out(DEPTH, 8)
            split_lo(dve, DEPTH, 19)
            attention_out(2)

            def memory_key_norms(n):
                pair = kx_t[:, 2 * n:2 * n + 2, :]
                head_norms(4 + n, [(pair, pair, N_MK, 0, 512)], 512)

            memory_key_norms(0)
            turned_out(DEPTH, 10)
            split_lo(dve, DEPTH, 20)
            attention_out(3)

            def over_norms(n):
                c = slice(2 * n, 2 * n + 2)
                dve.wait_ge(once["ab_root"], n + 1)
                then_next(dve.reciprocal(ab_stat[:, c], ab_stat[:, c]))
                src = a_tok if n == 0 else b_tok
                for i in range(TI):
                    dve.scalar_tensor_tensor(src[:, i], src[:, i], ab_stat[:, 2 * n + i:2 * n + i + 1], out_gain[:, n],
                                             ALU.mult, ALU.mult).then_inc(once["ab_scaled"], 1)

            dve.wait_ge(once["out_gain_loaded"], 16)
            over_norms(0)
            split_lo(dve, DEPTH, 21)
            over_norms(1)
            for b in range(4):
                o_rest(DEPTH, b, 4 * (b // 2), b % 2)
            memory_key_norms(1)
            for b in range(4):
                split_lo(dve, DEPTH, 22 + b)
                update(b, "w", 0, "slab_used", 20 + b)
                if b:
                    rests(b - 1, 16, N_MEM)
            rests(3, 16, N_MEM)
            inverse_root(DEPTH, 1, rstd[:, 0:T], root[:, 0:T])
            for n in range(2):
                dve.wait_ge(sig["slab_used"], v2("slab_used", 24 + n))
                dve.tensor_tensor(q_t[:, 2 * n:2 * n + 2, :], halves(bank(f"mq{n}", DEPTH)[:, :]),
                                  twice(rstd[:, 0:T]), ALU.mult).then_inc(once["mq_evac"], 1)
            for n in range(2):
                pair = q_t[:, 2 * n:2 * n + 2, :]
                head_norms(6 + n, [(pair, pair, N_MQ, 0, 512)], 512)
            for u in range(12, 16):
                dve.wait_ge(sig["scores"], v2("scores", u + 1))
                c = 32 + 2 * (u - 12)
                dve.tensor_reduce(neg_max[:, c:c + 2], halves(bank(f"scores{u}", DEPTH)[:, :]), AX.X, ALU.max,
                                  negate=True).then_inc(sig["neg_max"], 1)
            turned_out(DEPTH, 12)
            split_lo(dve, DEPTH, 26)
            turned_out(DEPTH, 14)
            split_lo(dve, DEPTH, 27)
            dve.wait_ge(once["b_sum"], 4)
            for i in range(TI):
                o_out(DEPTH, 4 + i, 13 + 2 * i, 32 + 4 * i, 4)
            for i in range(TI):
                o_rest(DEPTH, 4 + i, 0, i)
            for b in range(4):
                if b % 2 == 0:
                    update(b, "mo", 4, "first_bank", b // 2 + 1)
                else:
                    update(b, "mo", 4, "slab_used", 26 + b // 2)
                    split_lo(dve, DEPTH, 28 + b // 2)
                if b:
                    rests(b - 1, 24, N_FFN)
            rests(3, 24, N_FFN)
            inverse_root(DEPTH, 2, rstd[:, 0:T], root[:, 0:T])
            hidden_up(DEPTH, 28, 30)
            for b in range(4):
                for s in range(46 + 4 * b, min(50 + 4 * b, 59)):
                    split_lo(dve, DEPTH, s)
                update(b, "down", 8, "slab_used", 47 + 4 * b)

        @block.tensor
        def _(pe):
            def turn_rows(rows, first_bank):
                for b in range(4):
                    for k in range(2):
                        for i in range(TI):
                            ins = pe.transpose(banks[first_bank + b][:, T * k + P * i:T * k + P * i + P],
                                               rows[:, i, P * (2 * b + k):P * (2 * b + k) + P], ident)
                    ins.then_inc(i_turned, 1)

            pe.wait_ge(i_load["ident"], 16)
            pe.wait_ge(i_load["x"], 16)
            turn_rows(prologue_x, 0)
            pe.wait_ge(i_load["first_gain"], 16)
            for l in range(DEPTH):
                c = slice(P * (l + 1), P * (l + 2))
                ins = pe.transpose(banks[6][:, P * l:P * l + P], v_mla[:, 1, c], ident)
            ins.then_inc(i_turned, 1)
            pe.wait_ge(i_evac, 5)
            pe.wait_ge(i_scaled, TI)
            turn_rows(prologue_mem, 4)
            pe.wait_ge(i_load["gains"], 16 * 9)
            for l in range(DEPTH):
                ins = pe.transpose(banks[0][:, P * l:P * l + P], v_mla[:, 0, P * l:P * l + P], ident)
            ins.then_inc(i_turned, 1)
            pe.wait_ge(i_load["relb"], 16)
            pe.wait_ge(i_load["cst"], 16)
            pe.matmul(banks[1][0:HEADS, :], small[0:33, 0:HEADS], cst[0:33, C_ONEHOT:C_ONEHOT + 512],
                      start=True, stop=True).then_inc(i_turned, 1)
            pe.wait_ge(i_load["gains_2"], 16 * len(gain_rows_2(A)))
            pe.transpose(banks[2][:, 0:P], v_mla[:, 1, 0:P], ident).then_inc(i_turned, 1)
            pe.wait_ge(i_evac, 8)
            pe.wait_ge(i_mem_evac, 4)
            pe.wait_ge(i_clear, 3)

            def stat(layer, n):
                b = open_bank(pe, layer, f"stat{n}")
                if n == 1:
                    pe.wait_ge(sig["c_square"], value("c_square", layer, 1))
                    for half, (k0, k1) in enumerate(((0, 3), (3, 5))):
                        for k in range(k0, k1):
                            ins = pe.matmul(b[:, T * half:T * half + T], ones[:, :], kx_t[:, k, :],
                                            start=k == k0, stop=k == k1 - 1)
                    ins.then_inc(sig["stat_mm"], 1)
                    return
                sum_tokens(layer, b, n - (n > 1), n == 0)

            def sum_tokens(layer, b, norm, both):
                pe.wait_ge(sig["sumsq"], value("sumsq", layer, 2 * norm + 2))
                parts = [(src, a) for src in (sumsq, sq_next) for a in range(2)]
                for n, (src, a) in enumerate(parts):
                    if n == 2:
                        pe.wait_ge(sig["square"], value("square", layer, 4 * norm + 4))
                    ins = pe.matmul(b[:, 0:T], ones[:, :], src[:, T * a:T * a + T], start=n == 0, stop=n == 3)
                if both:
                    for i in range(TI):
                        for n, (src, a) in enumerate(parts):
                            ins = pe.matmul(b[:, T + i:T + i + 1], src[:, T * a + P * i:T * a + P * i + P],
                                            ones[:, 0:1], start=n == 0, stop=n == 3)
                ins.then_inc(sig["stat_mm"], 1)

            def scores(layer, u):
                b = open_bank(pe, layer, f"scores{u}")
                if u < 12:
                    i, heads, kt = unit(u % 6)
                    if u == 0:
                        pe.wait_ge(sig["z_evac"], value("z_evac", layer, 8))
                    if u == 6:
                        pe.wait_ge(sig["z_evac"], value("z_evac", layer, 16))
                        pe.wait_ge(sig["kpe"], value("kpe", layer, 1))
                    w = P * kt
                    for n, h in enumerate(heads):
                        o = b[:, w * n:w * n + w]
                        t = slice(P * i, P * i + P)
                        if u < 6:
                            r = slice(64 * (h % 2), 64 * (h % 2) + 64)
                            ins = pe.matmul(o, qk_dil[r, h // 2, t], qk_dil[r, 4 + h // 2, 0:w], start=True, stop=True)
                        else:
                            ins = pe.matmul(o, q_t[:, h, t], k_t[:, h, 0:w], start=True, stop=True)
                else:
                    i, heads = x_unit(u - 12)
                    pe.wait_ge(sig["z_evac"], value("z_evac", layer, 20))
                    for n, h in enumerate(heads):
                        for c in range(2):
                            ins = pe.matmul(b[:, T * n:T * n + T], q_t[:, 2 * h + c, P * i:P * i + P],
                                            kx_t[:, 2 * h + c, :], start=c == 0, stop=c == 1)
                ins.then_inc(sig["scores"], 1)

            def turn(layer, u):
                b = open_bank(pe, layer, f"turn{u}")
                pe.wait_ge(sig["probs"], value("probs", layer, u + 1))
                for n in range(4):
                    ins = pe.transpose(b[:, P * n:P * n + P], probs[:, u % P_RING, P * n:P * n + P], ident)
                ins.then_inc(sig["p_turned"], 1)

            def pv(layer, u):
                n, opens, _ = o_bank(u)
                b = open_bank(pe, layer, f"o{n}") if opens else bank(f"o{n}")
                name, count = pt_signal(u)
                pe.wait_ge(sig[name], value(name, layer, count))
                pt = p_t[:, u % PT_RING, :]
                if u < 12:
                    i, heads, kt = unit(u % 6)
                    if u in (0, 6):
                        pe.wait_ge(sig["v_evac"], value("v_evac", layer, 4 if u == 0 else 6))
                    v = v_dil if u < 6 else v_mla
                    for m, h in enumerate(heads):
                        for c in range(kt):
                            ins = pe.matmul(b[:, 64 * h:64 * h + 64], pt[:, P * (kt * m + c):P * (kt * m + c) + P],
                                            v[:, c, 64 * h:64 * h + 64], start=c == 0, stop=c == kt - 1)
                else:
                    i, heads = x_unit(u - 12)
                    for m, h in enumerate(heads):
                        for c in range(TI):
                            ins = pe.matmul(b[:, T * m:T * m + T], pt[:, P * (2 * m + c):P * (2 * m + c) + P],
                                            vx[:, c, T * h:T * h + T], start=c == 0, stop=c == 1)
                ins.then_inc(sig["pv"], 1)

            def turn_o(layer, n):
                b = open_bank(pe, layer, f"ot{n}")
                pe.wait_ge(sig["o_evac"], value("o_evac", layer, n + 1))
                for c in range(4):
                    ins = pe.transpose(b[:, P * c:P * c + P], o_tok[:, n % TI, P * c:P * c + P], ident)
                ins.then_inc(sig["o_turned"], 1)

            def slab(layer, s):
                names = [u for u, _, _ in slab_banks(s)]
                if s in (9, 10):
                    wh, wl = w_view(layer, s, 512)
                    pe.wait_ge(sig["slab_lo"], value("slab_lo", layer, s + 1))
                    pe.wait_ge(sig["c_lo"], value("c_lo", layer, 3))
                    for m in range(4):
                        if m % 2 == 0:
                            b = open_bank(pe, layer, names[m // 2])
                        o = b[:, T * (m % 2):T * (m % 2) + T]
                        for k in range(3):
                            c = slice(P * m, P * m + P)
                            ins = products3(pe, o, wh3(layer, s)[:, k, c], wl3(layer, s)[:, k, c], o_hi[:, k], o_lo[:, k],
                                            k == 0, k == 2)
                        if m == 1:
                            ins.then_inc(sig["first_bank"], 1)
                    ins.then_inc(sig["slab_used"], 1)
                elif s == 11:
                    pe.wait_ge(sig["slab_lo"], value("slab_lo", layer, s + 1))
                    pe.wait_ge(sig["c_lo"], value("c_lo", layer, 5))
                    wh = w_hi[:, slot(layer, s)].rearrange("p (a k n) -> p a k n", a=2, k=2)
                    wl = w_lo[:, slot(layer, s)].rearrange("p (a k n) -> p a k n", a=2, k=2)
                    for m in range(4):
                        if m % 2 == 0:
                            b = open_bank(pe, layer, names[m // 2])
                        o = b[:, T * (m % 2):T * (m % 2) + T]
                        for k in range(2):
                            c = slice(P * m, P * m + P)
                            ins = products3(pe, o, wh[:, 0, k, c], wl[:, 0, k, c], o_hi[:, 3 + k], o_lo[:, 3 + k],
                                            k == 0, k == 1)
                        if m % 2:
                            ins.then_inc(sig["first_bank"], 1)
                    for i in range(TI):
                        b = open_bank(pe, layer, names[2 + i])
                        t = slice(P * i, P * i + P)
                        for k in range(2):
                            ins = products3(pe, b[:, :], o_hi[:, 3 + k, t], o_lo[:, 3 + k, t], wh[:, 1, k], wl[:, 1, k],
                                            k == 0, k == 1)
                        ins.then_inc(sig["first_bank"] if i == 0 else sig["slab_used"], 1)
                elif s in (7, 8) or 16 <= s < 20:
                    rows_slab(pe, layer, s, open_bank(pe, layer, names[0]), act_hi, act_lo)
                elif s < 48:
                    b = open_bank(pe, layer, names[0])
                    wait = None
                    if s == 12:
                        def wait(k):
                            pe.wait_ge(sig["act_lo"], value("act_lo", layer, 8 + k + 1))
                    elif s in (20, 28):
                        pe.wait_ge(sig["o_lo"], value("o_lo", layer, 4 if s == 20 else 8))
                    from_o = 20 <= s < 24 or 28 <= s < 32
                    columns_slab(pe, layer, s, b, *((o_hi, o_lo) if from_o else (act_hi, act_lo)), ready=wait)
                else:
                    n, c = divmod(s - 48, 4)
                    b = open_bank(pe, layer, names[0]) if c == 0 else bank(f"down{n}")
                    if n == 0:
                        pe.wait_ge(sig["h_lo"], value("h_lo", layer, 4 * c + 4))
                    down_slab(layer, s, b, c)

            def down_slab(layer, s, b, c):
                pe.wait_ge(sig["slab_lo"], value("slab_lo", layer, s + 1))
                wh, wl = w_view(layer, s, 256)
                for m in range(2):
                    cs = slice(P * m, P * m + P)
                    for k in range(8):
                        ins = pe.matmul(b[:, T * m:T * m + T], wh[:, k, cs], h_hi[:, 8 * c + k],
                                        start=c == 0 and k == 0 and m == 0, stop=False, skip_group_check=True)
                        pe.matmul(b[:, T * m:T * m + T], wh[:, k, cs], h_lo[:, 8 * c + k],
                                  start=False, stop=False, skip_group_check=True)
                        ins = pe.matmul(b[:, T * m:T * m + T], wl[:, k, cs], h_hi[:, 8 * c + k],
                                        start=False, stop=c == 3 and k == 7, skip_group_check=True)
                ins.then_inc(sig["slab_used"], 1)

            def wh3(layer, s):
                return w_hi[:, slot(layer, s), 0:1536].rearrange("p (k n) -> p k n", k=3)

            def wl3(layer, s):
                return w_lo[:, slot(layer, s), 0:1536].rearrange("p (k n) -> p k n", k=3)

            def kpe(layer, _):
                b = open_bank(pe, layer, "kpe")
                pe.wait_ge(sig["z_evac"], value("z_evac", layer, 5))
                pe.matmul(b[:, 0:T], sel, latents[:, 5, :], start=True, stop=True).then_inc(sig["kpe_mm"], 1)

            def pair(layer, s):
                names = [slab_banks(s + n)[0][0] for n in range(2)]
                slab_pair(pe, layer, s, names, {0: 0, 24: 16, 32: 24}[s])

            steps = {"slab": slab, "pair": pair, "stat": stat, "kpe": kpe, "scores": scores, "turn": turn, "pv": pv, "ot": turn_o}
            with pe.Fori(0, DEPTH) as layer:
                for kind, n in TE_ORDER:
                    steps[kind](layer, n)
            def stat_2(n):
                b = open_bank(pe, DEPTH, f"stat{n}")
                sum_tokens(DEPTH, b, n, n == 0)

            def head_sums(n):
                b = open_bank(pe, DEPTH, f"hs{n}")
                pe.wait_ge(once["hs_square"], n + 1)
                w = 30 if n == 3 else 512
                over = cst[:, C_BLOCK:C_BLOCK + P] if n < 4 else ones[:, :]
                pe.matmul(b[:, 0:w], over, head_sq[:, n % 2, 0:w], start=True, stop=True).then_inc(once["hs_mm"], 1)

            def turn_token_weights(n):
                b = open_bank(pe, DEPTH, f"sgw{n}")
                pe.wait_ge(once["sgw_masked"], 1)
                for g in range(4):
                    ins = pe.transpose(b[:, P * g:P * g + P], sg_w[:, 4 * n + g], ident)
                ins.then_inc(once["sgw_turned"], 1)

            def turn_memory(n):
                b = open_bank(pe, DEPTH, f"mem{n}")
                pe.wait_ge(once["mem_scaled"], TI)
                for k in range(2):
                    for i in range(TI):
                        c = P * (2 * n + k)
                        ins = pe.transpose(b[:, T * k + P * i:T * k + P * i + P], mem_rows_2[:, i, c:c + P], ident)
                ins.then_inc(once["mem_turned"], 1)

            def turn_compressed_values(_):
                b = open_bank(pe, DEPTH, "vturn0")
                pe.wait_ge(once["kc_evac"], 3)
                for v in range(2):
                    ins = pe.transpose(b[:, P * v:P * v + P], c_z[:, v], ident)
                ins.then_inc(once["vturned"], 1)

            def compressed_scores(v):
                b = open_bank(pe, DEPTH, f"cscores{v}")
                pe.wait_ge(once["hs_done"], 4)
                r = slice(64 * v, 64 * v + 64)
                for i in range(TI):
                    for j in range(4):
                        c = 32 * (4 * i + j)
                        ins = pe.matmul(b[:, c:c + 32], q_t[r, j, P * i:P * i + P], kc[r, v], start=True, stop=True)
                ins.then_inc(once["c_scores"], 1)

            def turn_compressed(_):
                b = open_bank(pe, DEPTH, "cturn0")
                pe.wait_ge(once["c_exp"], 2)
                for v in range(2):
                    for i in range(TI):
                        c = P * (2 * v + i)
                        ins = pe.transpose(b[:, c:c + P], c_p[:, v, P * i:P * i + P], ident)
                ins.then_inc(once["c_turned"], 1)

            def compressed_pv(i):
                b = open_bank(pe, DEPTH, f"oc{i}")
                pe.wait_ge(once["cturn_evac"], 1)
                pe.wait_ge(once["vblk"], 1)
                for v in range(2):
                    ins = pe.matmul(b[:, T * v:T * v + T], c_pt[:, v, i], c_v[:, v], start=True, stop=True)
                ins.then_inc(once["c_pv"], 1)

            def spatial(i):
                b = open_bank(pe, DEPTH, f"sgu{i}")
                pe.wait_ge(once["ln_done"], 1)
                pe.wait_ge(once["sgw_evac"], 2)
                for g in range(8):
                    c = slice(64 * g, 64 * g + 64)
                    ins = pe.matmul(b[:, c], sg_w[:, g], v_dil[:, i, c], start=True, stop=True)
                ins.then_inc(once["sgu_mm"], 1)

            def scores_2(u):
                b = open_bank(pe, DEPTH, f"scores{u}")
                if u < 12:
                    i, heads, kt = unit_2(u % 6)
                    pe.wait_ge(once["hs_done"], 3)
                    for n, h in enumerate(heads):
                        v, j = divmod(h, 4)
                        w = P * kt
                        r = slice(64 * v, 64 * v + 64)
                        ins = pe.matmul(b[:, w * n:w * n + w], q_t[r, j, P * i:P * i + P], k_t[r, u // 6, 0:w],
                                        start=True, stop=True)
                else:
                    i, heads = x_unit(u - 12)
                    pe.wait_ge(once["hs_done"], 8)
                    for n, h in enumerate(heads):
                        ins = pe.matmul(b[:, T * n:T * n + T], q_t[:, h, P * i:P * i + P], kx_t[:, h, :],
                                        start=True, stop=True)
                ins.then_inc(sig["scores"], 1)

            def pv_2(u):
                n, opens, _ = o_bank_2(u)
                b = open_bank(pe, DEPTH, f"o{n}") if opens else bank(f"o{n}", DEPTH)
                name, count = pt_signal(u)
                pe.wait_ge(sig[name], v2(name, count))
                pt = p_t[:, u % PT_RING, :]
                if u < 12:
                    i, heads, kt = unit_2(u % 6)
                    pe.wait_ge(once["y_evac"], 3)
                else:
                    (i, heads), kt = x_unit(u - 12), TI
                    pe.wait_ge(once["mv_evac"], 2)
                for m, h in enumerate(heads):
                    for c in range(kt):
                        if u < 12:
                            w, v = 64, v_mla[:, c, P * (u // 6) + 64 * (h // 4):P * (u // 6) + 64 * (h // 4) + 64]
                        else:
                            w, v = P, mem_v[:, c, P * h:P * h + P]
                        ins = pe.matmul(b[:, w * h:w * h + w], pt[:, P * (kt * m + c):P * (kt * m + c) + P], v,
                                        start=c == 0, stop=c == kt - 1)
                ins.then_inc(sig["pv"], 1)

            def turn_o_2(n):
                b = open_bank(pe, DEPTH, f"ot{n}")
                if n < 4:
                    pe.wait_ge(once["ab_scaled"], n + 1)
                    src = (a_tok if n < 2 else b_tok)[:, n % 2]
                else:
                    pe.wait_ge(sig["o_evac"], v2("o_evac", n + 1))
                    src = o_tok[:, n % TI, :]
                for c in range(4):
                    ins = pe.transpose(b[:, P * c:P * c + P], src[:, P * c:P * c + P], ident)
                ins.then_inc(sig["o_turned"], 1)

            def turn_out(n):
                b = open_bank(pe, DEPTH, f"out{n}")
                pe.wait_ge(once["w_evac"], 9 + n)
                for i in range(TI):
                    for k in range(2):
                        c = T * i + P * k
                        ins = pe.transpose(b[:, c:c + P], x_t[:, 2 * n + k, P * i:P * i + P], ident)
                ins.then_inc(once["out_turned"], 1)

            def slab_2(s):
                names = [u for u, _, _ in slab_banks_2(s)]
                act_parts, o_parts = (act_hi, act_lo), (o_hi, o_lo)
                if s == 2:
                    b = open_bank(pe, DEPTH, names[0])
                    pe.wait_ge(sig["slab_lo"], v2("slab_lo", s + 1))
                    wh, wl = w_view(DEPTH, s, 256)
                    for k in range(8):
                        products3(pe, b[:, 0:T], wh[:, k, 0:P], wl[:, k, 0:P], act_hi[:, k], act_lo[:, k],
                                  k == 0, k == 7)
                    for i in range(TI):
                        t = slice(P * i, P * i + P)
                        for k in range(8):
                            ins = products3(pe, b[:, T + P * i:T + P * i + P], act_hi[:, k, t], act_lo[:, k, t],
                                            wh[:, k, P:2 * P], wl[:, k, P:2 * P], k == 0, k == 7)
                    ins.then_inc(sig["slab_used"], 1)
                elif 5 <= s < 9:
                    kind, half = divmod(s - 5, 2)
                    b = open_bank(pe, DEPTH, names[0]) if half == 0 else bank(f"ch{kind}", DEPTH)
                    pe.wait_ge(sig["slab_lo"], v2("slab_lo", s + 1))
                    pe.wait_ge(once["cin_lo"], 1)
                    wh, wl = w_view(DEPTH, s, 256)
                    for m in range(2):
                        c = slice(P * m, P * m + P)
                        o = b[:, 30 * m:30 * m + 30]
                        for k in range(8):
                            at = 480 * kind + 30 * (8 * half + k)
                            hi, lo = cin_hi[:, at:at + 30], cin_lo[:, at:at + 30]
                            pe.matmul(o, wh[:, k, c], hi, start=half + m + k == 0, stop=False, skip_group_check=True)
                            pe.matmul(o, wh[:, k, c], lo, start=False, stop=False, skip_group_check=True)
                            ins = pe.matmul(o, wl[:, k, c], hi, start=False, stop=half == 1 and k == 7,
                                            skip_group_check=True)
                    ins.then_inc(sig["slab_used"], 1)
                elif s == 9:
                    b = open_bank(pe, DEPTH, names[0])
                    pe.wait_ge(sig["slab_lo"], v2("slab_lo", s + 1))
                    pe.wait_ge(once["ch_lo"], 2)
                    wh = w_hi[:, slot(DEPTH, s), 0:512].rearrange("p (k n) -> p k n", n=P)
                    wl = w_lo[:, slot(DEPTH, s), 0:512].rearrange("p (k n) -> p k n", n=P)
                    for kind in range(2):
                        for k in range(2):
                            c = slice(60 * kind + 30 * k, 60 * kind + 30 * k + 30)
                            ins = products3(pe, b[:, 64 * kind:64 * kind + 30], wh[:, 2 * kind + k], wl[:, 2 * kind + k],
                                            ch_hi[:, c], ch_lo[:, c], k == 0, k == 1)
                    ins.then_inc(sig["slab_used"], 1)
                elif s == 10:
                    b = open_bank(pe, DEPTH, names[0])
                    pe.wait_ge(sig["slab_lo"], v2("slab_lo", s + 1))
                    wh = w_hi[:, slot(DEPTH, s), 0:192].rearrange("p (k n) -> p k n", n=24)
                    wl = w_lo[:, slot(DEPTH, s), 0:192].rearrange("p (k n) -> p k n", n=24)
                    for i in range(TI):
                        t = slice(P * i, P * i + P)
                        for k in range(8):
                            ins = products3(pe, b[:, 24 * i:24 * i + 24], act_hi[:, k, t], act_lo[:, k, t],
                                            wh[:, k], wl[:, k], k == 0, k == 7)
                    ins.then_inc(sig["slab_used"], 1)
                elif 11 <= s < 15 or 17 <= s < 19:
                    rows_slab(pe, DEPTH, s, open_bank(pe, DEPTH, names[0]), *act_parts)
                elif s in (25, 26):
                    wh, wl = w_view(DEPTH, s, 512)
                    pe.wait_ge(sig["slab_lo"], v2("slab_lo", s + 1))
                    pe.wait_ge(sig["o_lo"], v2("o_lo", 6))
                    for m in range(4):
                        if m % 2 == 0:
                            b = open_bank(pe, DEPTH, names[m // 2])
                        c = slice(P * m, P * m + P)
                        for k in range(4):
                            ins = products3(pe, b[:, T * (m % 2):T * (m % 2) + T], wh[:, k, c], wl[:, k, c],
                                            o_hi[:, k], o_lo[:, k], k == 0, k == 3)
                        if m % 2:
                            ins.then_inc(sig["first_bank" if m == 1 else "slab_used"], 1)
                elif s < 43:
                    wait = None
                    if s == 15:
                        def wait(k):
                            pe.wait_ge(sig["act_lo"], v2("act_lo", 8 + k + 1))
                    b = open_bank(pe, DEPTH, names[0])
                    if s == 19:
                        pe.wait_ge(sig["o_lo"], v2("o_lo", 4))
                    columns_slab(pe, DEPTH, s, b, *(o_parts if 19 <= s < 23 else act_parts), ready=wait)
                else:
                    n, c = divmod(s - 43, 4)
                    b = open_bank(pe, DEPTH, names[0]) if c == 0 else bank(f"down{n}", DEPTH)
                    if n == 0:
                        pe.wait_ge(sig["h_lo"], v2("h_lo", 4 * c + 4))
                    down_slab(DEPTH, s, b, c)

            def pair_2(s):
                names = [slab_banks_2(s + n)[0][0] for n in range(2)]
                slab_pair(pe, DEPTH, s, names, {0: 0, 23: 16, 27: 24}[s])

            steps_2 = {"slab": slab_2, "pair": pair_2, "stat": stat_2, "hs": head_sums, "sgw": turn_token_weights, "mem": turn_memory,
                       "vturn": turn_compressed_values, "cscores": compressed_scores, "cturn": turn_compressed,
                       "cpv": compressed_pv, "sgu": spatial, "scores": scores_2, "pv": pv_2, "ot": turn_o_2,
                       "turn": lambda u: turn(DEPTH, u), "out": turn_out}
            for kind, n in TE_ORDER_2:
                steps_2[kind](n)


def kernel(**inputs):
    from concourse import bacc
    from concourse.bass_utils import run_bass_kernel_spmd

    nc = bacc.Bacc("TRN2", target_bir_lowering=False, num_devices=1)
    inputs["shape_constants"] = shape_constants()
    arrays, A = {}, {}
    for name, a in inputs.items():
        a = np.ascontiguousarray(a)
        arrays[f"in_{name}_dram"] = a
        A[name] = nc.dram_tensor(f"in_{name}_dram", a.shape, mybir.dt.from_np(a.dtype), kind="ExternalInput").ap()
    out = nc.dram_tensor("out_dram", (1, T, D), F32, kind="ExternalOutput").ap()
    build(nc, A, out)
    result = run_bass_kernel_spmd(nc, [arrays], core_ids=[0])
    return result.results[0]["out_dram"]
```
